# Optimizing a Trainium2 kernel written in Bass

```python
import math
import jax, jax.numpy as jnp
from jax import lax
import numpy as np

D_MODEL = 1024
BATCH = 1
SEQ = 512
DEPTH = 1

CHUNK = 64
Q_BLOCK = 128

FOX_HEADS = 8
FOX_HEAD_DIM = 64
FOX_WIDTH = FOX_HEADS * FOX_HEAD_DIM

GLA_HEADS = 4
GLA_KEY_DIM = 128
GLA_VAL_DIM = 256
GLA_QK_WIDTH = GLA_HEADS * GLA_KEY_DIM
GLA_V_WIDTH = GLA_HEADS * GLA_VAL_DIM
GLA_GATE_RANK = 16
GLA_GATE_TEMP = 16.0
GLA_NORM_EPS = 1e-5

PEER_HEADS = 8
PEER_N_KEYS = 128
PEER_N_EXPERTS = PEER_N_KEYS * PEER_N_KEYS
PEER_QUERY_DIM = 256
PEER_HALF = PEER_QUERY_DIM // 2
PEER_TOPK = 16
PEER_TOKEN_BLOCK = 128

ALPHA = (2.0 * DEPTH) ** 0.25
BETA = (8.0 * DEPTH) ** -0.25
LN_EPS = 1e-5

IN_SPLIT_SIZES = (FOX_WIDTH, FOX_WIDTH, FOX_WIDTH, FOX_HEADS,
                  GLA_QK_WIDTH, GLA_QK_WIDTH, GLA_V_WIDTH, GLA_V_WIDTH, GLA_GATE_RANK,
                  D_MODEL, D_MODEL)
IN_WIDTH = sum(IN_SPLIT_SIZES)
IN_SPLIT_POINTS = tuple(int(v) for v in np.cumsum(IN_SPLIT_SIZES)[:-1])

kernel_name = "hybrid_fox_gla_peer_block"

def layer_norm(x, gain, bias):
    xf = x.astype(jnp.float32)
    mu = jnp.mean(xf, axis=-1, keepdims=True)
    var = jnp.mean(jnp.square(xf - mu), axis=-1, keepdims=True)
    y = (xf - mu) * lax.rsqrt(var + LN_EPS)
    return (y * gain.astype(jnp.float32) + bias.astype(jnp.float32)).astype(x.dtype)

def fox_attention(q, k, v, f_logit):
    B, S, H, dh = q.shape
    log_f = jax.nn.log_sigmoid(f_logit.astype(jnp.float32))
    c = jnp.cumsum(log_f, axis=1).transpose(0, 2, 1)
    scale = dh ** -0.5
    outs = []
    for i in range(S // Q_BLOCK):
        q0, q1 = i * Q_BLOCK, (i + 1) * Q_BLOCK
        qb, kb, vb = q[:, q0:q1], k[:, :q1], v[:, :q1]
        logits = jnp.einsum('bqhd,bkhd->bhqk', qb, kb).astype(jnp.float32) * scale
        logits = logits + c[:, :, q0:q1, None] - c[:, :, None, :q1]
        q_pos = jnp.arange(q0, q1)[:, None]
        k_pos = jnp.arange(q1)[None, :]
        logits = jnp.where(k_pos <= q_pos, logits, -jnp.inf)
        probs = jax.nn.softmax(logits, axis=-1).astype(v.dtype)
        outs.append(jnp.einsum('bhqk,bkhd->bqhd', probs, vb))
    return jnp.concatenate(outs, axis=1)

def gla_chunk_attention(q, k, v, log_a):
    B, S, H, dk = q.shape
    dv = v.shape[-1]
    nc = S // CHUNK

    def to_chunks(t):
        return t.reshape(B, nc, CHUNK, *t.shape[2:]).swapaxes(0, 1)

    la = to_chunks(log_a)
    cum = jnp.cumsum(la, axis=2)
    total = cum[:, :, -1]
    k_dec = to_chunks(k).astype(jnp.float32) * jnp.exp(total[:, :, None] - cum)
    qc = to_chunks(q).astype(jnp.float32)
    vc = to_chunks(v).astype(jnp.float32)

    def step(state, inp):
        q_c, k_c, v_c, tot = inp
        state = state * jnp.exp(tot)[..., None] + jnp.einsum('bchk,bchv->bhkv', k_c, v_c)
        o_c = jnp.einsum('bchk,bhkv->bchv', q_c, state)
        return state, o_c

    init = jnp.zeros((B, H, dk, dv), jnp.float32)
    _, o = lax.scan(step, init, (qc, k_dec, vc, total))
    return o.swapaxes(0, 1).reshape(B, S, H, dv)

def peer_layer(h, w_query, sub_keys, expert_u, expert_v):
    B, S, D = h.shape
    T = B * S
    ht = h.reshape(T, D)
    q = jnp.einsum('td,dhq->thq', ht, w_query).reshape(T, PEER_HEADS, 2, PEER_HALF)
    scores = jnp.einsum('thpc,hpnc->thpn', q, sub_keys).astype(jnp.float32)
    s_top, i_top = lax.top_k(scores, PEER_TOPK)
    cand = (s_top[:, :, 0, :, None] + s_top[:, :, 1, None, :]).reshape(T, PEER_HEADS, PEER_TOPK * PEER_TOPK)
    cand_idx = (i_top[:, :, 0, :, None] * PEER_N_KEYS + i_top[:, :, 1, None, :]).reshape(T, PEER_HEADS, PEER_TOPK * PEER_TOPK)
    best, pos = lax.top_k(cand, PEER_TOPK)
    expert_idx = jnp.take_along_axis(cand_idx, pos, axis=-1)
    gates = jax.nn.softmax(best, axis=-1).astype(h.dtype)

    nb = T // PEER_TOKEN_BLOCK
    hb = ht.reshape(nb, PEER_TOKEN_BLOCK, D)
    ib = expert_idx.reshape(nb, PEER_TOKEN_BLOCK, PEER_HEADS * PEER_TOPK)
    gb = gates.reshape(nb, PEER_TOKEN_BLOCK, PEER_HEADS * PEER_TOPK)

    def block(args):
        h_blk, i_blk, g_blk = args
        u = expert_u[i_blk]
        vv = expert_v[i_blk]
        act = jax.nn.gelu(jnp.einsum('td,tkd->tk', h_blk, u), approximate=False)
        return jnp.einsum('tk,tkd->td', act * g_blk, vv)

    out = lax.map(block, (hb, ib, gb))
    return out.reshape(B, S, D)

def setup_inputs(seed: int = 0) -> dict:
    key = jax.random.key(seed)
    ks = jax.random.split(key, 17)
    f32 = jnp.float32
    nrm = lambda k, shape: jax.random.normal(k, shape, f32)
    L = DEPTH
    return {
        "x": nrm(ks[0], (BATCH, SEQ, D_MODEL)),
        "w_in": nrm(ks[1], (L, D_MODEL, IN_WIDTH)) * D_MODEL ** -0.5,
        "fox_f_bias": 3.0 + 0.5 * nrm(ks[2], (L, FOX_HEADS)),
        "gla_gate_up": nrm(ks[3], (L, GLA_GATE_RANK, GLA_QK_WIDTH)) * GLA_GATE_RANK ** -0.5,
        "gla_gate_bias": 0.1 * nrm(ks[4], (L, GLA_QK_WIDTH)),
        "gla_norm_gain": 1.0 + 0.02 * nrm(ks[5], (L, GLA_HEADS, GLA_VAL_DIM)),
        "w_out_fox": nrm(ks[6], (L, FOX_WIDTH, D_MODEL)) * FOX_WIDTH ** -0.5,
        "w_out_gla": nrm(ks[7], (L, GLA_V_WIDTH, D_MODEL)) * GLA_V_WIDTH ** -0.5,
        "w_out": nrm(ks[8], (L, D_MODEL, D_MODEL)) * (D_MODEL ** -0.5 * BETA),
        "ln1_gain": 1.0 + 0.02 * nrm(ks[9], (L, D_MODEL)),
        "ln1_bias": 0.02 * nrm(ks[10], (L, D_MODEL)),
        "peer_w_query": nrm(ks[11], (L, D_MODEL, PEER_HEADS, PEER_QUERY_DIM)) * D_MODEL ** -0.5,
        "peer_sub_keys": nrm(ks[12], (L, PEER_HEADS, 2, PEER_N_KEYS, PEER_HALF)) * PEER_HALF ** -0.5,
        "peer_expert_u": nrm(ks[13], (L, PEER_N_EXPERTS, D_MODEL)) * D_MODEL ** -0.5,
        "peer_expert_v": nrm(ks[14], (L, PEER_N_EXPERTS, D_MODEL)) * BETA,
        "ln2_gain": 1.0 + 0.02 * nrm(ks[15], (L, D_MODEL)),
        "ln2_bias": 0.02 * nrm(ks[16], (L, D_MODEL)),
    }

def reference(x, w_in, fox_f_bias, gla_gate_up, gla_gate_bias, gla_norm_gain, w_out_fox, w_out_gla,
              w_out, ln1_gain, ln1_bias, peer_w_query, peer_sub_keys, peer_expert_u, peer_expert_v,
              ln2_gain, ln2_bias):
    B, S, D = x.shape
    for l in range(DEPTH):
        proj = jnp.einsum('bsd,de->bse', x, w_in[l])
        (fq, fk, fv, ff, gq, gk, gv, gg, glr, mga, mgb) = jnp.split(proj, IN_SPLIT_POINTS, axis=-1)

        y_fox = fox_attention(fq.reshape(B, S, FOX_HEADS, FOX_HEAD_DIM),
                              fk.reshape(B, S, FOX_HEADS, FOX_HEAD_DIM),
                              fv.reshape(B, S, FOX_HEADS, FOX_HEAD_DIM),
                              ff + fox_f_bias[l])
        y_fox = jnp.einsum('bsf,fd->bsd', y_fox.reshape(B, S, FOX_WIDTH), w_out_fox[l])

        log_a = jax.nn.log_sigmoid((glr @ gla_gate_up[l] + gla_gate_bias[l]).astype(jnp.float32)) / GLA_GATE_TEMP
        o = gla_chunk_attention((gq * GLA_KEY_DIM ** -0.5).reshape(B, S, GLA_HEADS, GLA_KEY_DIM),
                                gk.reshape(B, S, GLA_HEADS, GLA_KEY_DIM),
                                gv.reshape(B, S, GLA_HEADS, GLA_VAL_DIM),
                                log_a.reshape(B, S, GLA_HEADS, GLA_KEY_DIM))
        o = o * lax.rsqrt(jnp.mean(jnp.square(o), axis=-1, keepdims=True) + GLA_NORM_EPS) * gla_norm_gain[l].astype(jnp.float32)
        o = o.reshape(B, S, GLA_V_WIDTH).astype(x.dtype) * jax.nn.silu(gg)
        y_gla = jnp.einsum('bsv,vd->bsd', o, w_out_gla[l])

        merged = jax.nn.sigmoid(mga) * y_fox + jax.nn.sigmoid(mgb) * y_gla
        mix = jnp.einsum('bsd,de->bse', merged, w_out[l])
        x = layer_norm(ALPHA * x + mix, ln1_gain[l], ln1_bias[l])

        ffn = peer_layer(x, peer_w_query[l], peer_sub_keys[l], peer_expert_u[l], peer_expert_v[l])
        x = layer_norm(ALPHA * x + ffn, ln2_gain[l], ln2_bias[l])
    return x


_drawn_inputs = setup_inputs


def setup_inputs(seed=0):
    import zlib

    import numpy as np

    out = dict(_drawn_inputs(seed))
    spreads = {}
    factors = {'gla_norm_gain': 3.729, 'ln2_gain': 2.862, 'ln2_bias': 2.858}
    for name, (base, spread) in spreads.items():
        noise = np.random.default_rng([zlib.crc32(name.encode()), seed]).standard_normal(out[name].shape)
        drawn = base * np.exp(spread * noise) if base else spread * noise
        out[name] = __import__('jax').numpy.asarray(drawn.astype(out[name].dtype))
    for name, factor in factors.items():
        out[name] = (out[name] * factor).astype(out[name].dtype)
    return out
```

```python
from contextlib import ExitStack

import concourse.bass as bass
from concourse import mybir

ALU = mybir.AluOpType
ACT = mybir.ActivationFunctionType
AX = mybir.AxisListType
F32 = mybir.dt.float32
F32R = mybir.dt.float32r
BF16 = mybir.dt.bfloat16
U32 = mybir.dt.uint32

P = 128
D = 1024
S = 512
KC = D // P
TB = S // P
CHUNK = 64
NCH = S // CHUNK
FH, FD = 8, 64
GH, GK, GV = 4, 128, 256
GRANK = 16
GATE_TEMP = 16.0
PH = 8
NKEY = 128
TOPK = 16
HP = 2 * PH
ALPHA = 2.0 ** 0.25
EPS = 1e-5
NEG = -1e30
NEG_REPLACE = -3.0e38

QW = 1024
RING = 8
STAGE = 4
UNIT = 4
NUNIT = NKEY // UNIT
GB = 32
NGB = S // GB
KIB = 1024


def build(nc, xT, x, mix_stream, fox_stream, small_w, fox_f_bias, gate_up, gate_bias, gla_gain,
          ln1_gain, ln1_bias, ln2_gain, ln2_bias, keysT, expert_uT, expert_v, out):
    gate_dram = nc.dram_tensor("gate_scratch", [NUNIT, P, NGB, UNIT * GB], F32, kind="Internal").ap()

    with ExitStack() as ctx:
        origin = (nc.sbuf_base + 127) // 128 * 128
        ctx.enter_context(nc.sbuf_tensor("arena", [P, (411 * KIB // 2 + 128) // 4], F32))

        def at(name, shape, dt, kib):
            return nc.alloc_sbuf_tensor_at(name, shape, dt, offset=origin + int(kib * KIB))

        stage = at("stage", [P, STAGE, QW], F32, 0)
        w_hi = at("w_hi", [P, RING, QW], F32R, 16)
        w_lo = at("w_lo", [P, RING, QW], F32R, 48)
        x_hi = at("x_hi", [P, KC, S], F32R, 80)
        x_lo = at("x_lo", [P, KC, S], F32R, 96)
        Q = 112
        small_sb = at("small_sb", [P, KC, 24], F32, Q + 0)
        glrT = at("glrT", [GRANK + 1, S], F32, Q + 1)
        gate_up_sb = at("gate_up_sb", [GRANK + 1, GH * GK], F32, Q + 3)
        xT_raw = at("xT_raw", [P, KC, S], F32, Q + 48)
        f_hi = at("f_hi", [P, 4, S], F32R, Q + 0)
        f_lo = at("f_lo", [P, 4, S], F32R, Q + 8)
        fqT = at("fqT", [P, 4, S], F32, Q + 16)
        fkT = at("fkT", [P, 4, S], F32, Q + 24)
        fv = at("fv", [P, TB, 512], F32, Q + 32)
        kdec = at("kdec", [P, TB, 512], F32, Q + 40)
        gv = at("gv", [P, TB, D], F32, Q + 48)
        gqT = at("gqT", [P, GH, S], F32, Q + 64)
        la = at("la", [P, TB, 512], F32, Q + 72)
        probs = at("probs", [P, 3, S], F32, Q + 72)
        state = at("state", [P, 2, GH, GV], F32, Q + 16)
        o = at("o", [P, TB, D], F32, Q + 24)
        o_hi = at("o_hi", [P, KC, S], F32R, Q + 40)
        o_lo = at("o_lo", [P, KC, S], F32R, Q + 56)
        mT = at("mT", [P, KC, S], F32, Q + 16)
        sig_a = at("sig_a", [P, 2, S], F32, Q + 72)
        sig_b = at("sig_b", [P, 2, S], F32, Q + 76)
        m_hi = at("m_hi", [P, KC, S], F32R, Q + 40)
        m_lo = at("m_lo", [P, KC, S], F32R, Q + 56)
        x1 = at("x1", [P, TB, D], F32, Q + 0)
        acc = at("acc", [P, TB, D], F32, Q + 16)
        ln_g1 = at("ln_g1", [P, D], F32, Q + 72)
        ln_b1 = at("ln_b1", [P, D], F32, Q + 76)
        qT = at("qT", [P, HP, S], F32, Q + 32)
        keys = at("keys", [P, HP, NKEY], F32, Q + 64)
        score = at("score", [P, HP, NKEY], F32, Q + 72)
        cand = at("cand", [P, PH, TOPK * TOPK], F32, Q + 8)
        oh_j = at("oh_j", [P, 2, 4, NKEY], F32, Q + 72)
        oh_i = at("oh_i", [P, 2, 4, NKEY], F32, Q + 76)
        gstage = [at("gstage_a", [P, NKEY, GB], F32, Q + 32), at("gstage_b", [P, NKEY, GB], F32, Q + 48)]
        wt_hi = at("wt_hi", [P, UNIT, S], F32R, Q + 32)
        wt_lo = at("wt_lo", [P, UNIT, S], F32R, Q + 40)
        act = at("act", [P, UNIT, S], F32, Q + 48)
        gates = at("gates", [P, NGB, UNIT, GB], F32, Q + 56)
        ln_g2 = at("ln_g2", [P, D], F32, Q + 64)
        ln_b2 = at("ln_b2", [P, D], F32, Q + 68)
        E = Q + 80
        ident = at("ident", [P, P], F32, E)
        ident_b = at("ident_b", [P, P], BF16, E + 0.5)
        mask_b = at("mask_b", [P, P], BF16, E + 0.75)
        later = at("later", [P, P], F32, E + 1)
        iota_n = at("iota_n", [P, NKEY], F32, E + 1.5)
        tiny = at("tiny", [P, 256], F32, E + 2)
        head_sel = at("head_sel", [FH, FH, P], F32, E + 3)
        gla_gain_sb = at("gla_gain_sb", [P, D], F32, E + 3)
        cum = at("cum", [FH, S], F32, E + 7)
        logf = at("logf", [FH, S], F32, E + 9)
        logf2 = at("logf2", [FH, S], F32, E + 11)
        zero_row = at("zero_row", [FH, S], F32, Q + 72)
        tmp = at("tmp", [P, 2, S], F32, E + 9)
        pT = at("pT", [P, 2, S], F32, E + 9)
        top_v = at("top_v", [P, HP, TOPK], F32, E + 3)
        top_i = at("top_i", [P, HP, TOPK], U32, E + 4)
        top_if = at("top_if", [P, HP, TOPK], F32, E + 5)
        best = at("best", [P, PH, TOPK], F32, E + 6)
        pos = at("pos", [P, PH, TOPK], U32, E + 6.5)
        pos_i = at("pos_i", [P, 2, PH, TOPK], U32, E + 7)
        pos_f = at("pos_f", [P, 2, PH, TOPK], F32, E + 8)
        ijg = at("ijg", [P, 3, P], F32, E + 9)
        picks = at("picks", [P, 3, S], F32, Q + 0)
        iota_o = at("iota_o", [P, TOPK], F32, E + 11)

        stats = tiny[:, 0:48]
        ss = tiny[:, 48:64]
        rs = tiny[:, 64:80]
        etot = tiny[:, 80:112].rearrange("p (h c) -> p h c", h=GH)
        negmax = tiny[:, 112:144]
        psums = tiny[:, 144:176]
        recips = tiny[:, 176:208]
        chunk_ind = tiny[:, 208:210]
        eps_col = tiny[:, 210:211]
        mv = tiny[:, 212:220].rearrange("p (t s) -> p t s", t=TB)
        sd = tiny[:, 220:224]
        f_bias = tiny[0:FH, 224:225]
        gsum = tiny[:, 232:240]
        grec = tiny[:, 240:248]

        bank = [ctx.enter_context(nc.psum_tensor(f"bank{i}", [P, 512], F32)) for i in range(8)]

        def sem(name):
            return ctx.enter_context(nc.semaphore(name))

        landed = [sem(f"landed{i}") for i in range(STAGE)]
        slot_seen, hi_done, split_done, quarter_used = sem("slot_seen"), sem("hi_done"), sem("split_done"), sem("quarter_used")
        const_made, pool_step = sem("const_made"), sem("pool_step")
        xt_in, small_in, gate_up_in, bias_in, gla_gain_in, gain_in = sem("xt_in"), sem("small_in"), sem("gate_up_in"), sem("bias_in"), sem("gla_gain_in"), sem("gain_in")
        xt_hi, xt_split = sem("xt_hi"), sem("xt_split")
        small_done, glr_ready, ff_ready, cum_ready = sem("small_done"), sem("glr_ready"), sem("ff_ready"), sem("cum_ready")
        aux_done, proj_evac = sem("aux_done"), sem("proj_evac")
        soft_ready, la_ready, decay_ready, kdec_ready = sem("soft_ready"), sem("la_ready"), sem("decay_ready"), sem("kdec_ready")
        fox_logits, fox_max, fox_exp, fox_norm = sem("fox_logits"), sem("fox_max"), sem("fox_exp"), sem("fox_norm")
        fox_turned, fox_pT, fox_pv, fox_hi, fox_split = sem("fox_turned"), sem("fox_pT"), sem("fox_pv"), sem("fox_hi"), sem("fox_split")
        kv_done, state_done, o_read, o_evac = sem("kv_done"), sem("state_done"), sem("o_read"), sem("o_evac")
        rms_sqrt, silu_ready, o_gated = sem("rms_sqrt"), sem("silu_ready"), sem("o_gated")
        oT_done, oT_hi, oT_split = sem("oT_done"), sem("oT_hi"), sem("oT_split")
        sig_ready, merged, m_hi_done, m_split = sem("sig_ready"), sem("merged"), sem("m_hi_done"), sem("m_split")
        x_in, ln_var, ln_sqrt, x1_ready, acc_ready = sem("x_in"), sem("ln_var"), sem("ln_sqrt"), sem("x1_ready"), sem("acc_ready")
        x1T_done, x1T_hi, x1T_split = sem("x1T_done"), sem("x1T_hi"), sem("x1T_split")
        q_evac, keys_in = sem("q_evac"), sem("keys_in")
        sc_done, sc_evac, sc_used = sem("sc_done"), sem("sc_evac"), sem("sc_used")
        best_ready, gate_exp, picks_ready, picks_turned, picks_evac = sem("best_ready"), sem("gate_exp"), sem("picks_ready"), sem("picks_turned"), sem("picks_evac")
        oh_ready, gm_done, gm_evac, gstage_free, gm_written = sem("oh_ready"), sem("gm_done"), sem("gm_evac"), sem("gstage_free"), sem("gm_written")
        gates_in, gates_used = sem("gates_in"), sem("gates_used")
        z_done, gelu_done, wt_mul, wt_hi_done, wt_done = sem("z_done"), sem("gelu_done"), sem("wt_mul"), sem("wt_hi_done"), sem("wt_done")
        ffn_done, acc_done = sem("ffn_done"), sem("acc_done")
        ln2_in, ln2_var, ln2_sqrt, y_ready, y_out = sem("ln2_in"), sem("ln2_var"), sem("ln2_sqrt"), sem("y_ready"), sem("y_out")
        act_step, dve_step = sem("act_step"), sem("dve_step")

        n_proj = 9 * 4
        first_merge = n_proj
        first_wout = first_merge + 4 * KC
        first_query = first_wout + 8
        first_expert = first_query + HP
        assert first_expert % RING == UNIT
        PT_UNITS = ["fq", "fk", "z", "fv", "gk", "sfx", "gq", "tot", "gv0", "gv1"]
        AUX = ["z", "sfx", "tot"]
        STREAMED = [name for name in PT_UNITS if name not in AUX] + ["gg0", "gg1"]

        def wait_product(eng, name, r):
            if name in AUX:
                eng.wait_ge(aux_done, 4 * AUX.index(name) + r + 1)
            else:
                by_column = name in ("fq", "fk", "gq")
                eng.wait_ge(quarter_used, 4 * STREAMED.index(name) + (r + 1 if by_column else 4))

        block = ctx.enter_context(nc.Block())

        @block.sync
        def _(sp):
            def load(n, src, width=QW):
                if n >= STAGE:
                    sp.wait_ge(split_done, n - STAGE + 1)
                sp.dma_start(stage[:, n % STAGE, 0:width], src).then_inc(landed[n % STAGE], 16)

            sp.dma_start(xT_raw[:], xT).then_inc(xt_in, 16)
            n = m = 0
            for n in range(first_expert):
                if first_merge <= n < first_wout and (n - first_merge) % 4 == 3:
                    load(n, fox_stream[(n - first_merge) // 4], 512)
                else:
                    load(n, mix_stream[m])
                    m += 1
            for k in range(UNIT):
                load(first_expert + k, expert_uT[k])
            with sp.Fori(0, NGB // 2) as i:
                for half in range(2):
                    sp.wait_ge(gm_evac, i * 16 + (4 + 8 * (half + 1)))
                    sp.dma_start(gate_dram[:, :, bass.ds(2 * i + half, 1), :].rearrange("u p b c -> p u (b c)"),
                                 gstage[half][:, :, :].rearrange("p (u c) t -> p u (c t)", c=UNIT)).then_inc(gm_written, 16)
                    sp.wait_ge(gm_written, i * 32 + 16 * (half + 1))
                    sp.sem_inc(gstage_free, 1)
            with sp.Fori(0, NUNIT - 1) as u:
                for k in range(2 * UNIT):
                    sp.wait_ge(split_done, u * RING + (first_expert + UNIT + k - STAGE + 1))
                    src = (expert_uT[bass.ds(UNIT * u + (UNIT + k), 1), :, :] if k < UNIT
                           else expert_v[bass.ds(UNIT * u + (k - UNIT), 1), :, :])
                    sp.dma_start(stage[:, k % STAGE, :], src.rearrange("e p c -> p (e c)")).then_inc(landed[k % STAGE], 16)
            for k in range(UNIT):
                load(first_expert + UNIT + RING * (NUNIT - 1) + k, expert_v[UNIT * (NUNIT - 1) + k])
            for t in range(TB):
                sp.wait_ge(y_ready, t + 1)
                sp.dma_start(out[t * P:(t + 1) * P, :], acc[:, t, :]).then_inc(y_out, 16)
            sp.wait_ge(y_out, 16 * TB)

        @block.gpsimd
        def _(pool):
            steps = [0]

            def step(ins):
                steps[0] += 1
                ins.then_inc(pool_step, 1)
                pool.wait_ge(pool_step, steps[0])

            step(nc.gpsimd.memset(ident[:], 0.0))
            step(nc.gpsimd.memset(ident_b[:], 0.0))
            step(nc.gpsimd.memset(mask_b[:], 0.0))
            step(nc.gpsimd.memset(later[:], 1.0))
            step(nc.gpsimd.memset(head_sel[:], 0.0))
            step(nc.gpsimd.memset(glrT[:], 1.0))
            step(nc.gpsimd.memset(chunk_ind, 0.0))
            step(nc.gpsimd.memset(eps_col, EPS))
            step(nc.gpsimd.affine_select(out=ident[:], in_=ident[:], compare_op=ALU.not_equal, fill=1.0, base=0,
                                         pattern=[[-1, P]], channel_multiplier=1))
            step(nc.gpsimd.affine_select(out=ident_b[:], in_=ident_b[:], compare_op=ALU.not_equal, fill=1.0, base=0,
                                         pattern=[[-1, P]], channel_multiplier=1))
            step(nc.gpsimd.affine_select(out=mask_b[:], in_=mask_b[:], compare_op=ALU.is_ge, fill=NEG, base=0,
                                         pattern=[[-1, P]], channel_multiplier=1))
            step(nc.gpsimd.affine_select(out=later[:], in_=later[:], compare_op=ALU.is_ge, fill=0.0, base=-1,
                                         pattern=[[-1, P]], channel_multiplier=1))
            step(nc.gpsimd.memset(later[CHUNK:P, 0:CHUNK], 0.0))
            step(nc.gpsimd.memset(chunk_ind[0:CHUNK, 0:1], 1.0))
            step(nc.gpsimd.memset(chunk_ind[CHUNK:P, 1:2], 1.0))
            step(nc.gpsimd.affine_select(out=head_sel[:], in_=head_sel[:], compare_op=ALU.not_equal, fill=-1.0, base=0,
                                         pattern=[[-1, FH], [0, P]], channel_multiplier=1))
            nc.gpsimd.iota(iota_n[:], pattern=[[1, NKEY]], base=0, channel_multiplier=0,
                           allow_small_or_imprecise_dtypes=True).then_inc(const_made, 1)

            def split(n, slot, width):
                nc.gpsimd.tensor_copy(w_hi[:, slot, 0:width], stage[:, slot % STAGE, 0:width]).then_inc(hi_done, 1)
                pool.wait_ge(hi_done, n + 1)
                nc.gpsimd.tensor_tensor(w_lo[:, slot, 0:width], stage[:, slot % STAGE, 0:width],
                                        w_hi[:, slot, 0:width], ALU.subtract).then_inc(split_done, 1)

            for n in range(first_expert + UNIT):
                pool.wait_ge(landed[n % STAGE], 16 * (n // STAGE + 1))
                if n >= RING:
                    pool.wait_ge(quarter_used, n - RING + 1)
                fox = first_merge <= n < first_wout and (n - first_merge) % 4 == 3
                split(n, n % RING, 512 if fox else QW)
            first = first_expert + UNIT
            with pool.Fori(0, NUNIT - 1) as u:
                for k in range(RING):
                    n = u * RING + (first + k)
                    pool.wait_ge(landed[k % STAGE], u * 32 + 16 * ((first + k) // STAGE + 1))
                    pool.wait_ge(z_done, u * UNIT + (k % UNIT + 1))
                    if k >= UNIT:
                        pool.wait_ge(ffn_done, u * 8 + 8)
                    pool.sem_inc(slot_seen, 1)
                    split(n, k, QW)
            for k in range(UNIT):
                n = first + RING * (NUNIT - 1) + k
                pool.wait_ge(landed[n % STAGE], 16 * (n // STAGE + 1))
                pool.wait_ge(z_done, UNIT * (NUNIT - 1) + k + 1)
                split(n, n % RING, QW)

        @block.tensor
        def _(pe):
            mm, tr = nc.tensor.matmul, nc.tensor.transpose

            def mm3(dst, l_hi, l_lo, r_hi, r_lo, first, last):
                mm(dst, l_lo, r_hi, start=first, stop=False)
                mm(dst, l_hi, r_lo, start=False, stop=False)
                return mm(dst, l_hi, r_hi, start=False, stop=last)

            quarter = [0]

            def columns(dst, a_hi, a_lo, kc=KC):
                n = quarter[0]
                pe.wait_ge(split_done, n + 1)
                s = n % RING
                for k in range(kc):
                    c = slice(k * P, (k + 1) * P)
                    ins = mm3(dst, w_hi[:, s, c], w_lo[:, s, c], a_hi[:, k, :], a_lo[:, k, :], k == 0, k == kc - 1)
                quarter[0] += 1
                return ins.then_inc(quarter_used, 1)

            def rows(dsts, a_hi, a_lo):
                for q in range(4):
                    n = quarter[0]
                    pe.wait_ge(split_done, n + 1)
                    s = n % RING
                    for kk in range(2):
                        k = 2 * q + kk
                        c = slice(kk * 512, kk * 512 + 512)
                        for t in range(TB):
                            r = slice(t * P, (t + 1) * P)
                            ins = mm3(dsts[t][:], a_hi[:, k, r], a_lo[:, k, r], w_hi[:, s, c], w_lo[:, s, c],
                                      k == 0, k == KC - 1)
                    ins.then_inc(quarter_used, 1)
                    quarter[0] += 1
                return ins

            pe.wait_ge(xt_in, 16)
            pe.wait_ge(small_in, 16)
            for k in range(KC):
                ins = mm(bank[7][0:FH, :], small_sb[:, k, 0:FH], xT_raw[:, k, :], start=(k == 0), stop=(k == KC - 1))
            ins.then_inc(small_done, 1)
            for k in range(KC):
                ins = mm(bank[6][0:GRANK, :], small_sb[:, k, FH:FH + GRANK], xT_raw[:, k, :], start=(k == 0), stop=(k == KC - 1))
            ins.then_inc(small_done, 1)

            for u, name in enumerate(PT_UNITS):
                b = bank[4 * (u % 2):4 * (u % 2) + 4]
                if u == 0:
                    pe.wait_ge(xt_split, KC)
                if u == 1:
                    pe.wait_ge(glr_ready, 1)
                    pe.wait_ge(ff_ready, 1)
                if u >= 2:
                    pe.wait_ge(proj_evac, 4 * (u - 1))
                if name in ("fq", "fk", "gq"):
                    for c in range(4):
                        columns(b[c][:], x_hi, x_lo)
                elif name == "z":
                    pe.wait_ge(gate_up_in, 32)
                    for t in range(TB):
                        mm(b[t][:], glrT[:, t * P:(t + 1) * P], gate_up_sb[:], start=True, stop=True).then_inc(aux_done, 1)
                elif name == "sfx":
                    pe.wait_ge(la_ready, TB)
                    pe.wait_ge(const_made, 1)
                    for t in range(TB):
                        mm(b[t][:], later[:], la[:, t, :], start=True, stop=True).then_inc(aux_done, 1)
                elif name == "tot":
                    for h in range(GH):
                        for t in range(TB):
                            ins = mm(b[h][:, 2 * t:2 * t + 2], la[:, t, h * GK:(h + 1) * GK], chunk_ind,
                                     start=True, stop=True)
                        ins.then_inc(aux_done, 1)
                else:
                    rows(b, x_hi, x_lo)

            NS = FH * TB
            pe.wait_ge(proj_evac, 4 * len(PT_UNITS))
            pe.wait_ge(cum_ready, 1)

            def place(h):
                return 64 * (h % 2), h // 2

            for i in range(NS + 3):
                if i < NS:
                    h, qb = divmod(i, TB)
                    p0, c = place(h)
                    w = (qb + 1) * P
                    if i >= 3:
                        pe.wait_ge(fox_exp, i - 2)
                    L = bank[i % 3]
                    mm(L[:, 0:w], fqT[p0:p0 + 64, c, qb * P:w], fkT[p0:p0 + 64, c, 0:w], start=True, stop=False)
                    mm(L[:, qb * P:w], ident_b[:], mask_b[:], start=False, stop=False)
                    mm(L[:, 0:w], head_sel[:, h, :], cum[:, 0:w], start=False, stop=True).then_inc(fox_logits, 1)
                if 2 <= i < NS + 2:
                    s = i - 2
                    h, qb = divmod(s, TB)
                    pe.wait_ge(fox_norm, s + 1)
                    if s >= 2:
                        pe.wait_ge(fox_pT, s - 1)
                    for kb in range(qb + 1):
                        ins = tr(bank[3 + s % 2][:, kb * P:(kb + 1) * P], probs[:, s % 3, kb * P:(kb + 1) * P], ident[:])
                    ins.then_inc(fox_turned, 1)
                if i >= 3:
                    s = i - 3
                    h, qb = divmod(s, TB)
                    p0, c = place(h)
                    pe.wait_ge(fox_pT, s + 1)
                    if h % 2 == 0 and qb == 0 and c >= 2:
                        pe.wait_ge(fox_split, c - 1)
                    for kb in range(qb + 1):
                        ins = mm(bank[5 + c % 2][p0:p0 + 64, qb * P:(qb + 1) * P], fv[:, kb, h * FD:(h + 1) * FD],
                                 pT[:, s % 2, kb * P:(kb + 1) * P], start=(kb == 0), stop=(kb == qb))
                    ins.then_inc(fox_pv, 1)

            pe.wait_ge(kdec_ready, TB)
            pe.wait_ge(fox_split, 4)
            for c in range(NCH + 1):
                for h in range(GH):
                    if c < NCH:
                        t, p0 = c // 2, CHUNK * (c % 2)
                        if c >= 1:
                            pe.wait_ge(state_done, 4 * (c - 1) + h + 1)
                        mm(bank[h][:, 0:GV], kdec[p0:p0 + CHUNK, t, h * GK:(h + 1) * GK],
                           gv[p0:p0 + CHUNK, t, h * GV:(h + 1) * GV], start=True, stop=True).then_inc(kv_done, 1)
                    if c >= 1:
                        r = c - 1
                        t, p0 = r // 2, CHUNK * (r % 2)
                        if r % 2 == 0 and t >= 2 and h == 0:
                            pe.wait_ge(o_evac, t - 1)
                        pe.wait_ge(state_done, 4 * r + h + 1)
                        mm(bank[4 + 2 * (t % 2) + h // 2][p0:p0 + CHUNK, (h % 2) * GV:(h % 2 + 1) * GV],
                           gqT[:, h, r * CHUNK:(r + 1) * CHUNK], state[:, r % 2, h, :], start=True, stop=True).then_inc(o_read, 1)
            rows(bank[0:4], x_hi, x_lo)
            pe.wait_ge(o_evac, TB)
            rows(bank[4:8], x_hi, x_lo)
            for v in range(KC):
                if v == 0:
                    pe.wait_ge(o_gated, 8)
                if v >= 4:
                    pe.wait_ge(oT_split, v - 3)
                for t in range(TB):
                    ins = tr(bank[v % 4][:, t * P:(t + 1) * P], o[:, t, v * P:(v + 1) * P], ident[:])
                ins.then_inc(oT_done, 1)
            for d in range(KC):
                b = bank[4 * (d % 2):4 * (d % 2) + 4]
                if d == 0:
                    pe.wait_ge(oT_split, KC)
                if d >= 2:
                    pe.wait_ge(merged, d - 1)
                columns(b[0][:], x_hi, x_lo)
                columns(b[1][:], x_hi, x_lo)
                columns(b[2][:], o_hi, o_lo)
                columns(b[3][:], f_hi, f_lo, 4)
            pe.wait_ge(m_split, KC)
            rows(bank[0:4], m_hi, m_lo)
            rows(bank[4:8], m_hi, m_lo)
            for k in range(KC):
                if k == 0:
                    pe.wait_ge(x1_ready, TB)
                if k >= 4:
                    pe.wait_ge(x1T_split, k - 3)
                for t in range(TB):
                    ins = tr(bank[k % 4][:, t * P:(t + 1) * P], x1[:, t, k * P:(k + 1) * P], ident[:])
                ins.then_inc(x1T_done, 1)
            pe.wait_ge(x1T_split, KC)
            for c in range(HP):
                if c >= 4:
                    pe.wait_ge(q_evac, c - 3)
                columns(bank[4 + c % 4][:], x_hi, x_lo)
            pe.wait_ge(q_evac, HP)
            pe.wait_ge(keys_in, 16)

            def turn_picks(t):
                pe.wait_ge(picks_ready, t + 1)
                if t >= 2:
                    pe.wait_ge(picks_evac, t - 1)
                for a in range(3):
                    ins = tr(bank[4 + t % 2][:, a * P:(a + 1) * P], ijg[:, a, :], ident[:])
                ins.then_inc(picks_turned, 1)

            for t in range(TB):
                for g in range(4):
                    if t >= 1:
                        pe.wait_ge(sc_evac, 4 * (t - 1) + g + 1)
                    for j in range(4):
                        hp = 4 * g + j
                        ins = mm(bank[g][:, j * P:(j + 1) * P], qT[:, hp, t * P:(t + 1) * P], keys[:, hp, :],
                                 start=True, stop=True)
                    ins.then_inc(sc_done, 1)
                if t >= 1:
                    turn_picks(t - 1)
            turn_picks(TB - 1)

            pe.wait_ge(sc_evac, 4 * TB)
            pe.sem_inc(gm_done, 2)
            with pe.Fori(0, NGB // 2) as i:
                for g in range(16):
                    pe.wait_ge(oh_ready, i * 16 + (g + 1))
                    pe.wait_ge(gm_evac, i * 16 + (g + 1))
                    for j in range(4):
                        ins = mm(bank[g % 4][:, j * P:(j + 1) * P], oh_j[:, g % 2, j, :], oh_i[:, g % 2, j, :],
                                 start=True, stop=True)
                    ins.then_inc(gm_done, 1)

            def score_tile(k, n):
                pe.wait_ge(split_done, n)
                for c in range(KC):
                    w = slice(c * P, (c + 1) * P)
                    ins = mm3(bank[k][:], w_hi[:, UNIT + k, w], w_lo[:, UNIT + k, w], x_hi[:, c, :], x_lo[:, c, :],
                              c == 0, c == KC - 1)
                ins.then_inc(z_done, 1)

            def score_tile_b(k, n, zfree):
                pe.wait_ge(split_done, n)
                pe.wait_ge(gelu_done, zfree)
                for c in range(KC):
                    w = slice(c * P, (c + 1) * P)
                    ins = mm3(bank[k][:], w_hi[:, k, w], w_lo[:, k, w], x_hi[:, c, :], x_lo[:, c, :],
                              c == 0, c == KC - 1)
                ins.then_inc(z_done, 1)

            def combine(u, n, slot):
                pe.wait_ge(wt_done, u * UNIT + UNIT)
                pe.wait_ge(split_done, n + UNIT)
                for m in range(8):
                    t, half = divmod(m, 2)
                    pe.wait_ge(acc_done, u * 8 + (m + 1))
                    for k in range(UNIT):
                        r, c = slice(t * P, (t + 1) * P), slice(half * 512, half * 512 + 512)
                        ins = mm3(bank[4 + m % 4][:], wt_hi[:, k, r], wt_lo[:, k, r],
                                  w_hi[:, slot + k, c], w_lo[:, slot + k, c], k == 0, k == UNIT - 1)
                    ins.then_inc(ffn_done, 1)

            pe.wait_ge(gm_evac, NGB * 8 + 4)
            pe.sem_inc(ffn_done, 8)
            for k in range(UNIT):
                score_tile(k, first_expert + k + 1)
            with pe.Fori(0, NUNIT - 1) as u:
                for k in range(UNIT):
                    score_tile_b(k, u * RING + (first_expert + UNIT + k + 1), u * UNIT + (k + 1))
                combine(u, u * RING + (first_expert + RING), UNIT)
            combine(NUNIT - 1, first_expert + UNIT + RING * (NUNIT - 1), 0)

        @block.scalar
        def _(sc):
            act_f = nc.scalar.activation
            steps = [0]

            def step(ins):
                steps[0] += 1
                ins.then_inc(act_step, 1)
                sc.wait_ge(act_step, steps[0])

            sc.dma_start(small_sb[:], small_w).then_inc(small_in, 16)
            sc.dma_start(gate_up_sb[0:GRANK, :], gate_up).then_inc(gate_up_in, 16)
            sc.dma_start(gate_up_sb[GRANK:GRANK + 1, :], gate_bias).then_inc(gate_up_in, 16)
            sc.dma_start(f_bias, fox_f_bias.rearrange("a h -> h a")).then_inc(bias_in, 16)
            sc.wait_ge(xt_in, 16)
            for k in range(KC):
                act_f(x_hi[:, k, :], xT_raw[:, k, :], ACT.Copy).then_inc(xt_hi, 1)
            sc.wait_ge(const_made, 1)
            sc.wait_ge(small_done, 2)
            act_f(glrT[0:GRANK, :], bank[6][0:GRANK, :], ACT.Copy).then_inc(glr_ready, 1)
            sc.wait_ge(bias_in, 16)
            step(act_f(logf[:], bank[7][0:FH, :], ACT.Identity, bias=f_bias))
            step(act_f(logf2[:], logf[:], ACT.Abs))
            step(act_f(logf2[:], logf2[:], ACT.Exp, scale=-1.0))
            act_f(logf2[:], logf2[:], ACT.Ln, bias=1.0).then_inc(ff_ready, 1)

            for u, name in enumerate(PT_UNITS):
                for r in range(4):
                    b = bank[4 * (u % 2) + r]
                    wait_product(sc, name, r)
                    if name == "fq":
                        if r == 0:
                            sc.wait_ge(xt_split, KC)
                        act_f(fqT[:, r, :], b[:], ACT.Copy, scale=FD ** -0.5).then_inc(proj_evac, 1)
                    elif name == "fk":
                        act_f(fkT[:, r, :], b[:], ACT.Copy).then_inc(proj_evac, 1)
                    elif name == "fv":
                        act_f(fv[:, r, :], b[:], ACT.Copy).then_inc(proj_evac, 1)
                    elif name == "gk":
                        act_f(kdec[:, r, :], b[:], ACT.Copy).then_inc(proj_evac, 1)
                    elif name == "gq":
                        act_f(gqT[:, r, :], b[:], ACT.Copy, scale=GK ** -0.5).then_inc(proj_evac, 1)
                    elif name in ("gv0", "gv1"):
                        if r == 0 and name == "gv0":
                            sc.wait_ge(xt_split, KC)
                        c = 512 * (name == "gv1")
                        act_f(gv[:, r, c:c + 512], b[:], ACT.Copy).then_inc(proj_evac, 1)
                    elif name == "z":
                        if r == 0:
                            sc.wait_ge(cum_ready, 1)
                        if r >= 2:
                            sc.wait_ge(la_ready, r - 1)
                        step(act_f(la[:, r, :], b[:], ACT.Copy))
                        step(act_f(tmp[:, r % 2, :], la[:, r, :], ACT.Abs))
                        step(act_f(tmp[:, r % 2, :], tmp[:, r % 2, :], ACT.Exp, scale=-1.0))
                        act_f(tmp[:, r % 2, :], tmp[:, r % 2, :], ACT.Ln, bias=1.0).then_inc(proj_evac, 1)
                    elif name == "sfx":
                        if r == 0:
                            sc.wait_ge(la_ready, TB)
                        if r >= 2:
                            sc.wait_ge(kdec_ready, r - 1)
                        act_f(tmp[:, r % 2, :], b[:], ACT.Exp, scale=1.0 / GATE_TEMP).then_inc(proj_evac, 1)
                    elif name == "tot":
                        act_f(etot[:, r, :], b[:, 0:NCH], ACT.Exp, scale=1.0 / GATE_TEMP).then_inc(proj_evac, 1)

            NS = FH * TB
            sc.wait_ge(kdec_ready, TB)
            for i in range(NS + 4):
                if i < NS:
                    w = (i % TB + 1) * P
                    sc.wait_ge(fox_max, i + 1)
                    if i >= 3:
                        sc.wait_ge(fox_turned, i - 2)
                    act_f(probs[:, i % 3, 0:w], bank[i % 3][:, 0:w], ACT.Exp, bias=negmax[:, i:i + 1],
                          accum_out=psums[:, i:i + 1]).then_inc(fox_exp, 1)
                if 2 <= i < NS + 2:
                    s = i - 2
                    w = (s % TB + 1) * P
                    sc.wait_ge(fox_turned, s + 1)
                    if s >= 2:
                        sc.wait_ge(fox_pv, s - 1)
                    act_f(pT[:, s % 2, 0:w], bank[3 + s % 2][:, 0:w], ACT.Copy).then_inc(fox_pT, 1)
                if i >= 4 and (i - 4) % 8 == 7:
                    c = (i - 4) // 8
                    sc.wait_ge(fox_pv, i - 3)
                    act_f(f_hi[:, c, :], bank[5 + c % 2][:], ACT.Copy).then_inc(fox_hi, 1)

            sc.dma_start(gla_gain_sb[:], gla_gain.broadcast_to([P, D])).then_inc(gla_gain_in, 16)
            for t in range(TB):
                sc.wait_ge(o_read, 8 * (t + 1))
                if t >= 1:
                    sc.wait_ge(o_evac, t)
                for half in range(2):
                    b = bank[4 + 2 * (t % 2) + half]
                    act_f(o[:, t, half * 512:half * 512 + 512], b[:], ACT.Copy)
                    for j in range(2):
                        ins = act_f(tmp[:, half, j * GV:(j + 1) * GV], b[:, j * GV:(j + 1) * GV], ACT.Square,
                                    accum_out=ss[:, 4 * t + 2 * half + j:4 * t + 2 * half + j + 1])
                ins.then_inc(o_evac, 1)
            sc.wait_ge(o_evac, TB)
            act_f(rs, ss, ACT.Sqrt, bias=eps_col, scale=1.0 / GV).then_inc(rms_sqrt, 1)
            for r in range(8):
                wait_product(sc, f"gg{r // 4}", r % 4)
                if r >= 2:
                    sc.wait_ge(o_gated, r - 1)
                act_f(tmp[:, r % 2, :], bank[r][:], ACT.Silu).then_inc(silu_ready, 1)
            for v in range(KC):
                sc.wait_ge(oT_done, v + 1)
                act_f(o_hi[:, v, :], bank[v % 4][:], ACT.Copy).then_inc(oT_hi, 1)
            for d in range(KC):
                b = bank[4 * (d % 2):4 * (d % 2) + 4]
                if d >= 2:
                    sc.wait_ge(merged, d - 1)
                sc.wait_ge(quarter_used, first_merge + 4 * d + 1)
                act_f(sig_a[:, d % 2, :], b[0][:], ACT.Sigmoid).then_inc(sig_ready, 1)
                sc.wait_ge(quarter_used, first_merge + 4 * d + 2)
                act_f(sig_b[:, d % 2, :], b[1][:], ACT.Sigmoid).then_inc(sig_ready, 1)
            sc.wait_ge(quarter_used, first_wout)
            sc.dma_start(x1[:], x.rearrange("(t p) d -> p t d", p=P)).then_inc(x_in, 16)
            for d in range(KC):
                sc.wait_ge(merged, d + 1)
                act_f(m_hi[:, d, :], mT[:, d, :], ACT.Copy).then_inc(m_hi_done, 1)
            sc.dma_start(ln_g1[:], ln1_gain.broadcast_to([P, D])).then_inc(gain_in, 16)
            sc.dma_start(ln_b1[:], ln1_bias.broadcast_to([P, D])).then_inc(gain_in, 16)
            sc.wait_ge(ln_var, 1)
            act_f(sd, mv[:, :, 1], ACT.Sqrt, bias=eps_col).then_inc(ln_sqrt, 1)
            sc.wait_ge(quarter_used, first_query)
            sc.dma_start(keys[:], keysT).then_inc(keys_in, 16)
            for t in range(TB):
                sc.wait_ge(x1_ready, t + 1)
                act_f(acc[:, t, :], x1[:, t, :], ACT.Copy, scale=ALPHA).then_inc(acc_ready, 1)
            for k in range(KC):
                sc.wait_ge(x1T_done, k + 1)
                act_f(x_hi[:, k, :], bank[k % 4][:], ACT.Copy).then_inc(x1T_hi, 1)
            for c in range(HP):
                sc.wait_ge(quarter_used, first_query + c + 1)
                act_f(qT[:, c, :], bank[4 + c % 4][:], ACT.Copy).then_inc(q_evac, 1)

            def evac_picks(t):
                sc.wait_ge(picks_turned, t + 1)
                act_f(picks[:, :, t * P:(t + 1) * P],
                      bank[4 + t % 2][:, 0:3 * P].rearrange("p (a t) -> p a t", a=3), ACT.Copy).then_inc(picks_evac, 1)

            sc.wait_ge(acc_ready, TB)
            for t in range(TB):
                if t >= 1:
                    sc.wait_ge(sc_used, t)
                for g in range(4):
                    sc.wait_ge(sc_done, 4 * t + g + 1)
                    act_f(score[:, 4 * g:4 * g + 4, :],
                          bank[g][:].rearrange("p (a n) -> p a n", a=4), ACT.Copy).then_inc(sc_evac, 1)
                if t >= 1:
                    sc.wait_ge(best_ready, t)
                    act_f(ijg[:, 2, :], ijg[:, 2, :], ACT.Exp).then_inc(gate_exp, 1)
                    evac_picks(t - 1)
            sc.wait_ge(best_ready, TB)
            act_f(ijg[:, 2, :], ijg[:, 2, :], ACT.Exp).then_inc(gate_exp, 1)
            evac_picks(TB - 1)

            sc.sem_inc(gstage_free, 2)
            sc.sem_inc(gm_evac, 4)
            with sc.Fori(0, NGB // 2) as i:
                for g in range(16):
                    half = g // 8
                    if g % 8 == 0:
                        sc.wait_ge(gstage_free, i * 2 + (half + 1))
                    sc.wait_ge(gm_done, i * 16 + (g + 3))
                    t0 = 4 * (g % 8)
                    act_f(gstage[half][:, :, t0:t0 + 4],
                          bank[g % 4][:].rearrange("p (t i) -> p i t", t=4), ACT.Copy).then_inc(gm_evac, 1)

            def load_gates(u):
                sc.dma_start(gates[:].rearrange("p b c t -> p (b c t)"),
                             gate_dram[bass.ds(u, 1), :, :, :].rearrange("u p b c -> p (u b c)")).then_inc(gates_in, 16)

            sc.wait_ge(gm_written, 16 * NGB)
            load_gates(0)
            sc.dma_start(ln_g2[:], ln2_gain.broadcast_to([P, D])).then_inc(ln2_in, 16)
            sc.dma_start(ln_b2[:], ln2_bias.broadcast_to([P, D])).then_inc(ln2_in, 16)
            for k in range(UNIT):
                sc.wait_ge(z_done, k + 1)
                act_f(act[:, k, :], bank[k][:], ACT.Gelu).then_inc(gelu_done, 1)
            with sc.Fori(0, NUNIT - 1) as u:
                for k in range(UNIT):
                    sc.wait_ge(z_done, u * UNIT + (UNIT + k + 1))
                    sc.wait_ge(wt_done, u * UNIT + (k + 1))
                    act_f(act[:, k, :], bank[k][:], ACT.Gelu).then_inc(gelu_done, 1)
                load_gates(u + 1)
            sc.wait_ge(ln2_var, 1)
            act_f(sd, mv[:, :, 1], ACT.Sqrt, bias=eps_col).then_inc(ln2_sqrt, 1)

        @block.vector
        def _(dve):
            v = nc.vector
            steps = [0]

            def step(ins):
                steps[0] += 1
                ins.then_inc(dve_step, 1)
                dve.wait_ge(dve_step, steps[0])

            for k in range(KC):
                dve.wait_ge(xt_hi, k + 1)
                v.tensor_tensor(x_lo[:, k, :], xT_raw[:, k, :], x_hi[:, k, :], ALU.subtract).then_inc(xt_split, 1)
            step(v.memset(zero_row[:], 0.0))
            dve.wait_ge(ff_ready, 1)
            step(v.scalar_tensor_tensor(out=logf[:], in0=logf[:], scalar=0.0, in1=logf2[:], op0=ALU.min, op1=ALU.subtract))
            v.tensor_tensor_scan(cum[:], logf[:], zero_row[:], 0.0, ALU.add, ALU.add).then_inc(cum_ready, 1)
            for r in range(TB):
                dve.wait_ge(proj_evac, 8 + r + 1)
                v.scalar_tensor_tensor(out=la[:, r, :], in0=la[:, r, :], scalar=0.0, in1=tmp[:, r % 2, :],
                                       op0=ALU.min, op1=ALU.subtract).then_inc(la_ready, 1)
            for r in range(TB):
                dve.wait_ge(proj_evac, 20 + r + 1)
                v.tensor_tensor(kdec[:, r, :], kdec[:, r, :], tmp[:, r % 2, :], ALU.mult).then_inc(kdec_ready, 1)
            NS = FH * TB
            for i in range(NS + 4):
                if i < NS:
                    w = (i % TB + 1) * P
                    dve.wait_ge(fox_logits, i + 1)
                    v.tensor_reduce(negmax[:, i:i + 1], bank[i % 3][:, 0:w], AX.X, ALU.max, negate=True).then_inc(fox_max, 1)
                if 1 <= i < NS + 1:
                    s = i - 1
                    w = (s % TB + 1) * P
                    dve.wait_ge(fox_exp, s + 1)
                    step(v.reciprocal(recips[:, s:s + 1], psums[:, s:s + 1]))
                    v.tensor_scalar(probs[:, s % 3, 0:w], probs[:, s % 3, 0:w], recips[:, s:s + 1], None,
                                    ALU.mult).then_inc(fox_norm, 1)
                if i >= 4 and (i - 4) % 8 == 7:
                    c = (i - 4) // 8
                    dve.wait_ge(fox_hi, c + 1)
                    v.tensor_tensor(f_lo[:, c, :], bank[5 + c % 2][:], f_hi[:, c, :], ALU.subtract).then_inc(fox_split, 1)
            for c in range(NCH):
                for h in range(GH):
                    dve.wait_ge(kv_done, 4 * c + h + 1)
                    if c >= 2:
                        dve.wait_ge(o_read, 4 * (c - 2) + h + 1)
                    if c == 0:
                        v.tensor_copy(state[:, 0, h, :], bank[h][:, 0:GV]).then_inc(state_done, 1)
                    else:
                        dve.wait_ge(state_done, 4 * (c - 1) + h + 1)
                        v.scalar_tensor_tensor(out=state[:, c % 2, h, :], in0=state[:, 1 - c % 2, h, :],
                                               scalar=etot[:, h, c:c + 1], in1=bank[h][:, 0:GV],
                                               op0=ALU.mult, op1=ALU.add).then_inc(state_done, 1)
            dve.wait_ge(rms_sqrt, 1)
            step(v.reciprocal(rs, rs))
            dve.wait_ge(gla_gain_in, 16)
            for t in range(TB):
                for h in range(GH):
                    c = slice(h * GV, (h + 1) * GV)
                    ins = v.scalar_tensor_tensor(out=o[:, t, c], in0=o[:, t, c], scalar=rs[:, 4 * t + h:4 * t + h + 1],
                                                 in1=gla_gain_sb[:, c], op0=ALU.mult, op1=ALU.mult)
            step(ins)
            for r in range(8):
                dve.wait_ge(silu_ready, r + 1)
                half, t = divmod(r, TB)
                c = slice(half * 512, half * 512 + 512)
                v.tensor_tensor(o[:, t, c], o[:, t, c], tmp[:, r % 2, :], ALU.mult).then_inc(o_gated, 1)
            for k in range(KC):
                dve.wait_ge(oT_hi, k + 1)
                v.tensor_tensor(o_lo[:, k, :], bank[k % 4][:], o_hi[:, k, :], ALU.subtract).then_inc(oT_split, 1)
            for d in range(KC):
                b = bank[4 * (d % 2):4 * (d % 2) + 4]
                dve.wait_ge(sig_ready, 2 * d + 2)
                dve.wait_ge(quarter_used, first_merge + 4 * d + 4)
                v.tensor_tensor(sig_a[:, d % 2, :], sig_a[:, d % 2, :], b[3][:], ALU.mult)
                step(v.tensor_tensor(sig_b[:, d % 2, :], sig_b[:, d % 2, :], b[2][:], ALU.mult))
                v.tensor_tensor(mT[:, d, :], sig_a[:, d % 2, :], sig_b[:, d % 2, :], ALU.add).then_inc(merged, 1)
            for d in range(KC):
                dve.wait_ge(m_hi_done, d + 1)
                v.tensor_tensor(m_lo[:, d, :], mT[:, d, :], m_hi[:, d, :], ALU.subtract).then_inc(m_split, 1)
            dve.wait_ge(x_in, 16)
            for r in range(8):
                half, t = divmod(r, TB)
                dve.wait_ge(quarter_used, first_wout + 4 * (half + 1))
                c = slice(half * 512, half * 512 + 512)
                ins = v.scalar_tensor_tensor(out=x1[:, t, c], in0=x1[:, t, c], scalar=ALPHA, in1=bank[r][:],
                                             op0=ALU.mult, op1=ALU.add)
            step(ins)

            def norm_stats(src):
                for t in range(TB):
                    for half in range(2):
                        ins = v.bn_stats(stats[:, 12 * t + 6 * half:12 * t + 6 * half + 6], src[:, t, half * 512:half * 512 + 512])
                step(ins)
                for t in range(TB):
                    ins = v.bn_aggr(mv[:, t, :], stats[:, 12 * t:12 * t + 12])
                return ins

            def norm_apply(src, gain, bias, done):
                step(v.reciprocal(sd, sd))
                for t in range(TB):
                    step(v.tensor_scalar(src[:, t, :], src[:, t, :], mv[:, t, 0:1], sd[:, t:t + 1], ALU.subtract, ALU.mult))
                    step(v.tensor_tensor(src[:, t, :], src[:, t, :], gain[:], ALU.mult))
                    v.tensor_tensor(src[:, t, :], src[:, t, :], bias[:], ALU.add).then_inc(done, 1)

            norm_stats(x1).then_inc(ln_var, 1)
            dve.wait_ge(ln_sqrt, 1)
            dve.wait_ge(gain_in, 32)
            norm_apply(x1, ln_g1, ln_b1, x1_ready)
            for k in range(KC):
                dve.wait_ge(x1T_hi, k + 1)
                v.tensor_tensor(x_lo[:, k, :], bank[k % 4][:], x_hi[:, k, :], ALU.subtract).then_inc(x1T_split, 1)

            square = [P, PH, TOPK, TOPK]
            dve.wait_ge(acc_ready, TB)
            v.tensor_copy(iota_o[:], iota_n[:, 0:TOPK])
            for t in range(TB):
                dve.wait_ge(sc_evac, 4 * t + 4)

                def top16(vals, idx, src, rows_n):
                    for a in range(rows_n):
                        ins = v.max(vals[:, a, 0:8], src[:, a, :])
                    step(ins)
                    for a in range(rows_n):
                        ins = v.max_index(idx[:, a, 0:8], vals[:, a, 0:8], src[:, a, :])
                    step(ins)
                    for a in range(rows_n):
                        ins = v.match_replace(src[:, a, :], vals[:, a, 0:8], src[:, a, :], NEG_REPLACE)
                    step(ins)
                    for a in range(rows_n):
                        ins = v.max(vals[:, a, 8:16], src[:, a, :])
                    step(ins)
                    for a in range(rows_n):
                        ins = v.max_index(idx[:, a, 8:16], vals[:, a, 8:16], src[:, a, :])
                    return ins

                top16(top_v, top_i, score, HP).then_inc(sc_used, 1)
                dve.wait_ge(sc_used, t + 1)
                v.tensor_copy(top_if[:], top_i[:])
                tv = top_v[:].rearrange("p (h s) k -> p h s k", s=2)
                step(v.tensor_tensor(
                    cand[:].rearrange("p h (a b) -> p h a b", a=TOPK),
                    tv[:, :, 0, :].unsqueeze(3).broadcast_to(square), tv[:, :, 1, :].unsqueeze(2).broadcast_to(square), ALU.add))
                step(top16(best, pos, cand, PH))
                if t >= 1:
                    dve.wait_ge(picks_turned, t)
                v.tensor_tensor(ijg[:, 2, :].rearrange("p (h k) -> p h k", h=PH), best[:],
                                best[:, :, 0:1].broadcast_to([P, PH, TOPK]), ALU.subtract).then_inc(best_ready, 1)
                v.tensor_scalar(pos_i[:, 0, :, :], pos[:], 4, None, ALU.logical_shift_right)
                step(v.tensor_scalar(pos_i[:, 1, :, :], pos[:], TOPK - 1, None, ALU.bitwise_and))
                step(v.tensor_copy(pos_f[:], pos_i[:]))
                ti = top_if[:].rearrange("p (h s) k -> p h s k", s=2)
                eq = cand[:].rearrange("p h (k o) -> p h k o", o=TOPK)
                for a in range(2):
                    step(v.tensor_tensor(eq, pos_f[:, a, :, :].unsqueeze(3).broadcast_to(square),
                                         iota_o[:].unsqueeze(1).unsqueeze(1).broadcast_to(square), ALU.is_equal))
                    step(v.tensor_tensor(eq, eq, ti[:, :, a, :].unsqueeze(2).broadcast_to(square), ALU.mult))
                    step(v.tensor_reduce(ijg[:, a, :].rearrange("p (h k) -> p h k", h=PH), eq, AX.X, ALU.add))
                dve.wait_ge(gate_exp, t + 1)
                gx = ijg[:, 2, :].rearrange("p (h k) -> p h k", h=PH)
                step(v.tensor_reduce(gsum, gx, AX.X, ALU.add))
                step(v.reciprocal(grec, gsum))
                v.tensor_tensor(gx, gx, grec.unsqueeze(2).broadcast_to([P, PH, TOPK]), ALU.mult).then_inc(picks_ready, 1)

            dve.wait_ge(picks_evac, TB)
            with dve.Fori(0, NGB // 2) as i:
                for g in range(16):
                    dve.wait_ge(gm_done, i * 16 + (g + 1))
                    for j in range(4):
                        tok = i * 64 + (4 * g + j)
                        v.tensor_scalar(oh_j[:, g % 2, j, :], iota_n[:], picks[:, 1, bass.ds(tok, 1)], None, ALU.is_equal)
                        ins = v.tensor_scalar(oh_i[:, g % 2, j, :], iota_n[:], picks[:, 0, bass.ds(tok, 1)],
                                              picks[:, 2, bass.ds(tok, 1)], ALU.is_equal, ALU.mult)
                    ins.then_inc(oh_ready, 1)

            def weigh(u, k):
                n = u * UNIT + (k + 1)
                dve.wait_ge(gelu_done, n)
                a = act[:, k, :]
                v.tensor_tensor(a.rearrange("p (b t) -> p b t", b=NGB), a.rearrange("p (b t) -> p b t", b=NGB),
                                gates[:, :, k, :], ALU.mult).then_inc(wt_mul, 1)
                dve.wait_ge(wt_mul, n)
                v.tensor_copy(wt_hi[:, k, :], a).then_inc(wt_hi_done, 1)
                dve.wait_ge(wt_hi_done, n)
                v.tensor_tensor(wt_lo[:, k, :], a, wt_hi[:, k, :], ALU.subtract).then_inc(wt_done, 1)

            def add_out(u, m):
                t, half = divmod(m, 2)
                c = slice(half * 512, half * 512 + 512)
                dve.wait_ge(ffn_done, u * 8 + (m + 9))
                v.tensor_tensor(acc[:, t, c], acc[:, t, c], bank[4 + m % 4][:], ALU.add).then_inc(acc_done, 1)

            dve.wait_ge(gates_in, 16)
            for k in range(UNIT):
                weigh(0, k)
            dve.sem_inc(acc_done, 4)
            with dve.Fori(0, NUNIT - 1) as u:
                for m in range(8):
                    dve.wait_ge(acc_done, u * 8 + (m + 1))
                    add_out(u, m)
                dve.wait_ge(gates_in, u * 16 + 32)
                for k in range(UNIT):
                    weigh(u + 1, k)
            for m in range(8):
                add_out(NUNIT - 1, m)
            dve.wait_ge(acc_done, 8 * NUNIT + 4)
            norm_stats(acc).then_inc(ln2_var, 1)
            dve.wait_ge(ln2_sqrt, 1)
            dve.wait_ge(ln2_in, 32)
            norm_apply(acc, ln_g2, ln_b2, y_ready)


def kernel(**inputs):
    import numpy as np
    import concourse.bacc as bacc
    from concourse.bass_utils import run_bass_kernel_spmd

    def of(name):
        return np.ascontiguousarray(inputs[name])[0]

    x = of("x")
    w_in = of("w_in")
    widths = [512, 512, 512, FH, GH * GK, GH * GK, D, D, GRANK, D, D]
    at = [sum(widths[:i]) for i in range(len(widths))]
    fq, fk, fv, ff, gq, gk, gv, gg, glr, mga, mgb = [w_in[:, a:a + n] for a, n in zip(at, widths)]

    def columns(w, c):
        k = w.shape[0] // P
        return w[:, c * P:(c + 1) * P].reshape(k, P, P).transpose(1, 0, 2).reshape(P, k * P)

    def rows(w, half, q):
        return w[2 * P * q:2 * P * (q + 1), 512 * half:512 * half + 512].reshape(2, P, 512).transpose(1, 0, 2).reshape(P, 1024)

    quarters = [columns(fq, c) for c in range(4)] + [columns(fk, c) for c in range(4)]
    quarters += [rows(fv, 0, q) for q in range(4)] + [rows(gk, 0, q) for q in range(4)]
    quarters += [columns(gq, c) for c in range(4)]
    quarters += [rows(w, half, q) for w in (gv, gg) for half in range(2) for q in range(4)]
    w_gla, w_fox, w_out = of("w_out_gla"), of("w_out_fox"), of("w_out")
    for d in range(D // P):
        quarters += [columns(mga, d), columns(mgb, d), columns(w_gla, d)]
    quarters += [rows(w_out, half, q) for half in range(2) for q in range(4)]
    w_query = of("peer_w_query").reshape(D, HP * P)
    quarters += [columns(w_query, c) for c in range(HP)]

    arrays = {
        "xT": x.reshape(S, KC, P).transpose(2, 1, 0),
        "x": x.reshape(S, D),
        "mix_stream": np.stack(quarters),
        "fox_stream": np.stack([columns(w_fox, d) for d in range(D // P)]),
        "small_w": np.concatenate([ff, glr], axis=1).reshape(KC, P, FH + GRANK).transpose(1, 0, 2),
        "fox_f_bias": of("fox_f_bias")[None],
        "gate_up": of("gla_gate_up"),
        "gate_bias": of("gla_gate_bias")[None],
        "gla_gain": of("gla_norm_gain").reshape(1, D),
        "ln1_gain": of("ln1_gain")[None], "ln1_bias": of("ln1_bias")[None],
        "ln2_gain": of("ln2_gain")[None], "ln2_bias": of("ln2_bias")[None],
        "keysT": of("peer_sub_keys").reshape(HP, NKEY, P).transpose(2, 0, 1),
        "expert_uT": of("peer_expert_u").reshape(NKEY, NKEY, KC, P).transpose(0, 3, 2, 1).reshape(NKEY, P, D),
        "expert_v": of("peer_expert_v").reshape(NKEY, NKEY, D),
    }
    arrays = {k: np.ascontiguousarray(a) for k, a in arrays.items()}
    nc = bacc.Bacc("TRN2", target_bir_lowering=False, num_devices=1)
    args = {k: nc.dram_tensor(f"in_{k}", a.shape, mybir.dt.from_np(a.dtype), kind="ExternalInput").ap()
            for k, a in arrays.items()}
    out = nc.dram_tensor("out_0", (S, D), F32, kind="ExternalOutput").ap()
    build(nc, out=out, **args)
    r = run_bass_kernel_spmd(nc, [{f"in_{k}": a for k, a in arrays.items()}], core_ids=[0])
    return r.results[0]["out_0"].reshape(1, S, D)
```

```python
from contextlib import ExitStack

import concourse.bass as bass
from concourse import mybir

ALU = mybir.AluOpType
ACT = mybir.ActivationFunctionType
AX = mybir.AxisListType
F32 = mybir.dt.float32
F32R = mybir.dt.float32r
BF16 = mybir.dt.bfloat16
U32 = mybir.dt.uint32

P = 128
D = 1024
S = 512
KC = D // P
TB = S // P
CHUNK = 64
NCH = S // CHUNK
FH, FD = 8, 64
GH, GK, GV = 4, 128, 256
GRANK = 16
GATE_TEMP = 16.0
PH = 8
NKEY = 128
TOPK = 16
HP = 2 * PH
ALPHA = 2.0 ** 0.25
EPS = 1e-5
NEG = -1e30
NEG_REPLACE = -3.0e38

QW = 1024
RING = 8
STAGE = 4
UNIT = 4
NUNIT = NKEY // UNIT
GB = 32
TOPK_TILES = 8
GATE_TILES = 8
NGB = S // GB
KIB = 1024


def build(nc, xT, x, mix_stream, fox_stream, small_w, fox_f_bias, gate_up, gate_bias, gla_gain,
          ln1_gain, ln1_bias, ln2_gain, ln2_bias, keysT, expert_uT, expert_v, out):
    gate_dram = nc.dram_tensor("gate_scratch", [NUNIT, P, NGB, UNIT * GB], F32, kind="Internal").ap()
    act_dram = nc.dram_tensor("activation_scratch", [NUNIT, P, UNIT, S], F32, kind="Internal").ap()

    with ExitStack() as ctx:
        origin = (nc.sbuf_base + 127) // 128 * 128
        ctx.enter_context(nc.sbuf_tensor("arena", [P, (411 * KIB // 2 + 128) // 4], F32))

        def at(name, shape, dt, kib):
            return nc.alloc_sbuf_tensor_at(name, shape, dt, offset=origin + int(kib * KIB))

        stage = at("stage", [P, STAGE, QW], F32, 0)
        w_hi = at("w_hi", [P, RING, QW], F32R, 16)
        w_lo = at("w_lo", [P, RING, QW], F32R, 48)
        x_hi = at("x_hi", [P, KC, S], F32R, 80)
        x_lo = at("x_lo", [P, KC, S], F32R, 96)
        Q = 112
        small_sb = at("small_sb", [P, KC, 24], F32, Q + 0)
        glrT = at("glrT", [GRANK + 1, S], F32, Q + 1)
        gate_up_sb = at("gate_up_sb", [GRANK + 1, GH * GK], F32, Q + 3)
        xT_raw = at("xT_raw", [P, KC, S], F32, Q + 48)
        f_hi = at("f_hi", [P, 4, S], F32R, Q + 0)
        f_lo = at("f_lo", [P, 4, S], F32R, Q + 8)
        fqT = at("fqT", [P, 4, S], F32, Q + 16)
        fkT = at("fkT", [P, 4, S], F32, Q + 24)
        fv = at("fv", [P, TB, 512], F32, Q + 32)
        kdec = at("kdec", [P, TB, 512], F32, Q + 40)
        gv = at("gv", [P, TB, D], F32, Q + 48)
        gqT = at("gqT", [P, GH, S], F32, Q + 64)
        la = at("la", [P, TB, 512], F32, Q + 72)
        probs = at("probs", [P, 3, S], F32, Q + 72)
        state = at("state", [P, 2, GH, GV], F32, Q + 16)
        o = at("o", [P, TB, D], F32, Q + 24)
        o_hi = at("o_hi", [P, KC, S], F32R, Q + 40)
        o_lo = at("o_lo", [P, KC, S], F32R, Q + 56)
        mT = at("mT", [P, KC, S], F32, Q + 16)
        sig_a = at("sig_a", [P, 2, S], F32, Q + 72)
        sig_b = at("sig_b", [P, 2, S], F32, Q + 76)
        m_hi = at("m_hi", [P, KC, S], F32R, Q + 40)
        m_lo = at("m_lo", [P, KC, S], F32R, Q + 56)
        x1 = at("x1", [P, TB, D], F32, Q + 0)
        acc = at("acc", [P, TB, D], F32, Q + 16)
        ln_g1 = at("ln_g1", [P, D], F32, Q + 72)
        ln_b1 = at("ln_b1", [P, D], F32, Q + 76)
        qT = at("qT", [P, HP, S], F32, Q + 32)
        keys = at("keys", [P, HP, NKEY], F32, Q + 64)
        score = at("score", [P, HP, NKEY], F32, Q + 72)
        cand = at("cand", [P, PH, TOPK * TOPK], F32, Q + 8)
        oh_j = at("oh_j", [P, 2, 4, NKEY], F32R, Q + 72)
        gate_parts = at("gate_parts", [P, 2, S], F32R, Q + 76)
        oh_hi = at("oh_hi", [P, 2, 4, NKEY], F32R, Q + 8)
        oh_lo = at("oh_lo", [P, 2, 4, NKEY], F32R, Q + 12)
        gstage = [at("gstage_a", [P, NKEY, GB], F32, Q + 32), at("gstage_b", [P, NKEY, GB], F32, Q + 48)]
        wt_hi = at("wt_hi", [P, 2, UNIT, S], F32R, Q + 32)
        wt_lo = at("wt_lo", [P, 2, UNIT, S], F32R, Q + 48)
        act = at("act", [P, UNIT, S], F32, Q + 64)
        gates = at("gates", [P, NGB, UNIT, GB], F32, Q + 72)
        ln_g2 = at("ln_g2", [P, D], F32, Q + 8)
        ln_b2 = at("ln_b2", [P, D], F32, Q + 12)
        E = Q + 80
        ident = at("ident", [P, P], F32, E)
        ident_b = at("ident_b", [P, P], BF16, E + 0.5)
        mask_b = at("mask_b", [P, P], BF16, E + 0.75)
        later = at("later", [P, P], F32, E + 1)
        iota_n = at("iota_n", [P, NKEY], F32, E + 1.5)
        tiny = at("tiny", [P, 256], F32, E + 2)
        head_sel = at("head_sel", [FH, FH, P], F32, E + 3)
        gla_gain_sb = at("gla_gain_sb", [P, D], F32, E + 3)
        cum = at("cum", [FH, S], F32, E + 7)
        logf = at("logf", [FH, S], F32, E + 9)
        logf2 = at("logf2", [FH, S], F32, E + 11)
        zero_row = at("zero_row", [FH, S], F32, Q + 72)
        tmp = at("tmp", [P, 2, S], F32, E + 9)
        pT = at("pT", [P, 2, S], F32, E + 9)
        top_v = at("top_v", [P, HP, TOPK], F32, E + 3)
        top_i = at("top_i", [P, HP, TOPK], U32, E + 4)
        top_if = at("top_if", [P, HP, TOPK], F32, E + 5)
        best = at("best", [P, PH, TOPK], F32, E + 6)
        pos = at("pos", [P, PH, TOPK], U32, E + 6.5)
        pos_i = at("pos_i", [P, 2, PH, TOPK], U32, E + 7)
        pos_f = at("pos_f", [P, 2, PH, TOPK], F32, E + 8)
        ijg = at("ijg", [P, 3, P], F32, E + 9)
        picks = at("picks", [P, 3, S], F32, Q + 0)
        iota_o = at("iota_o", [P, TOPK], F32, E + 10.5)
        act_out = [at("act_out_a", [P, S], F32, Q + 6), at("act_out_b", [P, S], F32, E + 11)]

        stats = tiny[:, 0:48]
        ss = tiny[:, 48:64]
        rs = tiny[:, 64:80]
        etot = tiny[:, 80:112].rearrange("p (h c) -> p h c", h=GH)
        negmax = tiny[:, 112:144]
        psums = tiny[:, 144:176]
        recips = tiny[:, 176:208]
        chunk_ind = tiny[:, 208:210]
        eps_col = tiny[:, 210:211]
        mv = tiny[:, 212:220].rearrange("p (t s) -> p t s", t=TB)
        sd = tiny[:, 220:224]
        f_bias = tiny[0:FH, 224:225]
        gsum = tiny[:, 232:240]
        grec = tiny[:, 240:248]

        bank = [ctx.enter_context(nc.psum_tensor(f"bank{i}", [P, 512], F32)) for i in range(8)]

        def sem(name):
            return ctx.enter_context(nc.semaphore(name))

        landed = [sem(f"landed{i}") for i in range(STAGE)]
        hi_done, split_done, quarter_used = sem("hi_done"), sem("split_done"), sem("quarter_used")
        const_made, pool_step = sem("const_made"), sem("pool_step")
        xt_in, small_in, gate_up_in, bias_in, gla_gain_in, gain_in = sem("xt_in"), sem("small_in"), sem("gate_up_in"), sem("bias_in"), sem("gla_gain_in"), sem("gain_in")
        xt_hi, xt_split = sem("xt_hi"), sem("xt_split")
        small_done, glr_ready, ff_ready, cum_ready = sem("small_done"), sem("glr_ready"), sem("ff_ready"), sem("cum_ready")
        aux_done, proj_evac = sem("aux_done"), sem("proj_evac")
        soft_ready, la_ready, decay_ready, kdec_ready = sem("soft_ready"), sem("la_ready"), sem("decay_ready"), sem("kdec_ready")
        fox_logits, fox_max, fox_exp, fox_norm = sem("fox_logits"), sem("fox_max"), sem("fox_exp"), sem("fox_norm")
        fox_turned, fox_pT, fox_pv, fox_hi, fox_split = sem("fox_turned"), sem("fox_pT"), sem("fox_pv"), sem("fox_hi"), sem("fox_split")
        kv_done, state_done, o_read, o_evac = sem("kv_done"), sem("state_done"), sem("o_read"), sem("o_evac")
        rms_sqrt, silu_ready, o_gated = sem("rms_sqrt"), sem("silu_ready"), sem("o_gated")
        oT_done, oT_hi, oT_split = sem("oT_done"), sem("oT_hi"), sem("oT_split")
        sig_ready, merged, m_hi_done, m_split = sem("sig_ready"), sem("merged"), sem("m_hi_done"), sem("m_split")
        x_in, ln_var, ln_sqrt, x1_ready, acc_ready = sem("x_in"), sem("ln_var"), sem("ln_sqrt"), sem("x1_ready"), sem("acc_ready")
        x1T_done, x1T_hi, x1T_split = sem("x1T_done"), sem("x1T_hi"), sem("x1T_split")
        q_evac, keys_in = sem("q_evac"), sem("keys_in")
        sc_done, sc_evac, sc_used = sem("sc_done"), sem("sc_evac"), sem("sc_used")
        best_ready, gate_exp, picks_ready, picks_turned, picks_evac = sem("best_ready"), sem("gate_exp"), sem("picks_ready"), sem("picks_turned"), sem("picks_evac")
        gate_split, oh_ready, gm_done, gm_evac = sem("gate_split"), sem("oh_ready"), sem("gm_done"), sem("gm_evac")
        gm_written = [sem("gm_written_a"), sem("gm_written_b")]
        act_written = [sem("act_written_a"), sem("act_written_b")]
        gates_in, act_in = sem("gates_in"), sem("act_in")
        gelu_done, wt_mul, wt_hi_done, wt_done = sem("gelu_done"), sem("wt_mul"), sem("wt_hi_done"), sem("wt_done")
        ffn_done, acc_done = sem("ffn_done"), sem("acc_done")
        ln2_in, ln2_var, ln2_sqrt, y_ready, y_out = sem("ln2_in"), sem("ln2_var"), sem("ln2_sqrt"), sem("y_ready"), sem("y_out")
        act_step, dve_step = sem("act_step"), sem("dve_step")

        n_proj = 9 * 4
        first_merge = n_proj
        first_wout = first_merge + 4 * KC
        first_query = first_wout + 8
        first_expert = first_query + HP
        ahead_tiles = TOPK_TILES * TB + GATE_TILES * (NGB // 2)
        ahead_units = ahead_tiles // UNIT
        mixed_units = NUNIT - ahead_units
        first_gate = first_expert + TOPK_TILES * TB
        first_mixed = first_expert + ahead_tiles
        first_tail = first_mixed + 2 * UNIT * mixed_units
        for n in (first_expert, first_gate, first_mixed, first_tail):
            assert n % RING == UNIT
        assert GATE_TILES == RING and mixed_units % 2 == 0
        PT_UNITS = ["fq", "fk", "z", "fv", "gk", "sfx", "gq", "tot", "gv0", "gv1"]
        AUX = ["z", "sfx", "tot"]
        STREAMED = [name for name in PT_UNITS if name not in AUX] + ["gg0", "gg1"]

        def wait_product(eng, name, r):
            if name in AUX:
                eng.wait_ge(aux_done, 4 * AUX.index(name) + r + 1)
            else:
                by_column = name in ("fq", "fk", "gq")
                eng.wait_ge(quarter_used, 4 * STREAMED.index(name) + (r + 1 if by_column else 4))

        block = ctx.enter_context(nc.Block())

        @block.sync
        def _(sp):
            def load(n, src, width=QW):
                if n >= STAGE:
                    sp.wait_ge(split_done, n - STAGE + 1)
                sp.dma_start(stage[:, n % STAGE, 0:width], src).then_inc(landed[n % STAGE], 16)

            sp.dma_start(xT_raw[:], xT).then_inc(xt_in, 16)
            n = m = 0
            for n in range(first_expert):
                if first_merge <= n < first_wout and (n - first_merge) % 4 == 3:
                    load(n, fox_stream[(n - first_merge) // 4], 512)
                else:
                    load(n, mix_stream[m])
                    m += 1
            for k in range(TOPK_TILES * TB):
                load(first_expert + k, expert_uT[k])

            def load_in_loop(n, k, src):
                sp.wait_ge(split_done, n - (STAGE - 1))
                sp.dma_start(stage[:, k % STAGE, :], src.rearrange("e p c -> p (e c)")).then_inc(landed[k % STAGE], 16)

            with sp.Fori(0, NGB // 2) as i:
                for k in range(GATE_TILES):
                    load_in_loop(i * RING + (first_gate + k), k,
                                 expert_uT[bass.ds(i * GATE_TILES + (TOPK_TILES * TB + k), 1), :, :])
            with sp.Fori(0, mixed_units) as u:
                for k in range(UNIT):
                    load_in_loop(u * RING + (first_mixed + k), k, expert_uT[bass.ds(u * UNIT + (ahead_tiles + k), 1), :, :])
                for k in range(UNIT):
                    load_in_loop(u * RING + (first_mixed + UNIT + k), k, expert_v[bass.ds(u * UNIT + k, 1), :, :])
            with sp.Fori(0, (NUNIT - mixed_units) // 2) as i:
                for k in range(RING):
                    load_in_loop(i * RING + (first_tail + k), k, expert_v[bass.ds(i * RING + (UNIT * mixed_units + k), 1), :, :])
            for t in range(TB):
                sp.wait_ge(y_ready, t + 1)
                sp.dma_start(out[t * P:(t + 1) * P, :], acc[:, t, :]).then_inc(y_out, 16)
            sp.wait_ge(y_out, 16 * TB)

        @block.gpsimd
        def _(pool):
            steps = [0]

            def step(ins):
                steps[0] += 1
                ins.then_inc(pool_step, 1)
                pool.wait_ge(pool_step, steps[0])

            step(nc.gpsimd.memset(ident[:], 0.0))
            step(nc.gpsimd.memset(ident_b[:], 0.0))
            step(nc.gpsimd.memset(mask_b[:], 0.0))
            step(nc.gpsimd.memset(later[:], 1.0))
            step(nc.gpsimd.memset(head_sel[:], 0.0))
            step(nc.gpsimd.memset(glrT[:], 1.0))
            step(nc.gpsimd.memset(chunk_ind, 0.0))
            step(nc.gpsimd.memset(eps_col, EPS))
            step(nc.gpsimd.affine_select(out=ident[:], in_=ident[:], compare_op=ALU.not_equal, fill=1.0, base=0,
                                         pattern=[[-1, P]], channel_multiplier=1))
            step(nc.gpsimd.affine_select(out=ident_b[:], in_=ident_b[:], compare_op=ALU.not_equal, fill=1.0, base=0,
                                         pattern=[[-1, P]], channel_multiplier=1))
            step(nc.gpsimd.affine_select(out=mask_b[:], in_=mask_b[:], compare_op=ALU.is_ge, fill=NEG, base=0,
                                         pattern=[[-1, P]], channel_multiplier=1))
            step(nc.gpsimd.affine_select(out=later[:], in_=later[:], compare_op=ALU.is_ge, fill=0.0, base=-1,
                                         pattern=[[-1, P]], channel_multiplier=1))
            step(nc.gpsimd.memset(later[CHUNK:P, 0:CHUNK], 0.0))
            step(nc.gpsimd.memset(chunk_ind[0:CHUNK, 0:1], 1.0))
            step(nc.gpsimd.memset(chunk_ind[CHUNK:P, 1:2], 1.0))
            step(nc.gpsimd.affine_select(out=head_sel[:], in_=head_sel[:], compare_op=ALU.not_equal, fill=-1.0, base=0,
                                         pattern=[[-1, FH], [0, P]], channel_multiplier=1))
            nc.gpsimd.iota(iota_n[:], pattern=[[1, NKEY]], base=0, channel_multiplier=0,
                           allow_small_or_imprecise_dtypes=True).then_inc(const_made, 1)

            def split_low(n, slot, width):
                pool.wait_ge(hi_done, n + 1)
                nc.gpsimd.tensor_tensor(w_lo[:, slot, 0:width], stage[:, slot % STAGE, 0:width],
                                        w_hi[:, slot, 0:width], ALU.subtract).then_inc(split_done, 1)

            for n in range(first_expert + UNIT):
                fox = first_merge <= n < first_wout and (n - first_merge) % 4 == 3
                split_low(n, n % RING, 512 if fox else QW)
            start = first_expert + UNIT
            total = first_expert + 2 * NKEY
            with pool.Fori(0, (total - start) // RING) as i:
                for k in range(RING):
                    split_low(i * RING + (start + k), k, QW)
            for n in range(start + (total - start) // RING * RING, total):
                split_low(n, n % RING, QW)

        @block.tensor
        def _(pe):
            mm, tr = nc.tensor.matmul, nc.tensor.transpose

            def mm3(dst, l_hi, l_lo, r_hi, r_lo, first, last):
                mm(dst, l_lo, r_hi, start=first, stop=False)
                mm(dst, l_hi, r_lo, start=False, stop=False)
                return mm(dst, l_hi, r_hi, start=False, stop=last)

            quarter = [0]

            def columns(dst, a_hi, a_lo, kc=KC):
                n = quarter[0]
                pe.wait_ge(split_done, n + 1)
                s = n % RING
                for k in range(kc):
                    c = slice(k * P, (k + 1) * P)
                    ins = mm3(dst, w_hi[:, s, c], w_lo[:, s, c], a_hi[:, k, :], a_lo[:, k, :], k == 0, k == kc - 1)
                quarter[0] += 1
                return ins.then_inc(quarter_used, 1)

            def rows(dsts, a_hi, a_lo):
                for q in range(4):
                    n = quarter[0]
                    pe.wait_ge(split_done, n + 1)
                    s = n % RING
                    for kk in range(2):
                        k = 2 * q + kk
                        c = slice(kk * 512, kk * 512 + 512)
                        for t in range(TB):
                            r = slice(t * P, (t + 1) * P)
                            ins = mm3(dsts[t][:], a_hi[:, k, r], a_lo[:, k, r], w_hi[:, s, c], w_lo[:, s, c],
                                      k == 0, k == KC - 1)
                    ins.then_inc(quarter_used, 1)
                    quarter[0] += 1
                return ins

            pe.wait_ge(xt_in, 16)
            pe.wait_ge(small_in, 16)
            for k in range(KC):
                ins = mm(bank[7][0:FH, :], small_sb[:, k, 0:FH], xT_raw[:, k, :], start=(k == 0), stop=(k == KC - 1))
            ins.then_inc(small_done, 1)
            for k in range(KC):
                ins = mm(bank[6][0:GRANK, :], small_sb[:, k, FH:FH + GRANK], xT_raw[:, k, :], start=(k == 0), stop=(k == KC - 1))
            ins.then_inc(small_done, 1)

            for u, name in enumerate(PT_UNITS):
                b = bank[4 * (u % 2):4 * (u % 2) + 4]
                if u == 0:
                    pe.wait_ge(xt_split, KC)
                if u == 1:
                    pe.wait_ge(glr_ready, 1)
                    pe.wait_ge(ff_ready, 1)
                if u >= 2:
                    pe.wait_ge(proj_evac, 4 * (u - 1))
                if name in ("fq", "fk", "gq"):
                    for c in range(4):
                        columns(b[c][:], x_hi, x_lo)
                elif name == "z":
                    pe.wait_ge(gate_up_in, 32)
                    for t in range(TB):
                        mm(b[t][:], glrT[:, t * P:(t + 1) * P], gate_up_sb[:], start=True, stop=True).then_inc(aux_done, 1)
                elif name == "sfx":
                    pe.wait_ge(la_ready, TB)
                    pe.wait_ge(const_made, 1)
                    for t in range(TB):
                        mm(b[t][:], later[:], la[:, t, :], start=True, stop=True).then_inc(aux_done, 1)
                elif name == "tot":
                    for h in range(GH):
                        for t in range(TB):
                            ins = mm(b[h][:, 2 * t:2 * t + 2], la[:, t, h * GK:(h + 1) * GK], chunk_ind,
                                     start=True, stop=True)
                        ins.then_inc(aux_done, 1)
                else:
                    rows(b, x_hi, x_lo)

            NS = FH * TB
            pe.wait_ge(proj_evac, 4 * len(PT_UNITS))
            pe.wait_ge(cum_ready, 1)

            def place(h):
                return 64 * (h % 2), h // 2

            for i in range(NS + 3):
                if i < NS:
                    h, qb = divmod(i, TB)
                    p0, c = place(h)
                    w = (qb + 1) * P
                    if i >= 3:
                        pe.wait_ge(fox_exp, i - 2)
                    L = bank[i % 3]
                    mm(L[:, 0:w], fqT[p0:p0 + 64, c, qb * P:w], fkT[p0:p0 + 64, c, 0:w], start=True, stop=False)
                    mm(L[:, qb * P:w], ident_b[:], mask_b[:], start=False, stop=False)
                    mm(L[:, 0:w], head_sel[:, h, :], cum[:, 0:w], start=False, stop=True).then_inc(fox_logits, 1)
                if 2 <= i < NS + 2:
                    s = i - 2
                    h, qb = divmod(s, TB)
                    pe.wait_ge(fox_norm, s + 1)
                    if s >= 2:
                        pe.wait_ge(fox_pT, s - 1)
                    for kb in range(qb + 1):
                        ins = tr(bank[3 + s % 2][:, kb * P:(kb + 1) * P], probs[:, s % 3, kb * P:(kb + 1) * P], ident[:])
                    ins.then_inc(fox_turned, 1)
                if i >= 3:
                    s = i - 3
                    h, qb = divmod(s, TB)
                    p0, c = place(h)
                    pe.wait_ge(fox_pT, s + 1)
                    if h % 2 == 0 and qb == 0 and c >= 2:
                        pe.wait_ge(fox_split, c - 1)
                    for kb in range(qb + 1):
                        ins = mm(bank[5 + c % 2][p0:p0 + 64, qb * P:(qb + 1) * P], fv[:, kb, h * FD:(h + 1) * FD],
                                 pT[:, s % 2, kb * P:(kb + 1) * P], start=(kb == 0), stop=(kb == qb))
                    ins.then_inc(fox_pv, 1)

            pe.wait_ge(kdec_ready, TB)
            pe.wait_ge(fox_split, 4)
            for c in range(NCH + 1):
                for h in range(GH):
                    if c < NCH:
                        t, p0 = c // 2, CHUNK * (c % 2)
                        if c >= 1:
                            pe.wait_ge(state_done, 4 * (c - 1) + h + 1)
                        mm(bank[h][:, 0:GV], kdec[p0:p0 + CHUNK, t, h * GK:(h + 1) * GK],
                           gv[p0:p0 + CHUNK, t, h * GV:(h + 1) * GV], start=True, stop=True).then_inc(kv_done, 1)
                    if c >= 1:
                        r = c - 1
                        t, p0 = r // 2, CHUNK * (r % 2)
                        if r % 2 == 0 and t >= 2 and h == 0:
                            pe.wait_ge(o_evac, t - 1)
                        pe.wait_ge(state_done, 4 * r + h + 1)
                        mm(bank[4 + 2 * (t % 2) + h // 2][p0:p0 + CHUNK, (h % 2) * GV:(h % 2 + 1) * GV],
                           gqT[:, h, r * CHUNK:(r + 1) * CHUNK], state[:, r % 2, h, :], start=True, stop=True).then_inc(o_read, 1)
            rows(bank[0:4], x_hi, x_lo)
            pe.wait_ge(o_evac, TB)
            rows(bank[4:8], x_hi, x_lo)
            for v in range(KC):
                if v == 0:
                    pe.wait_ge(o_gated, 8)
                if v >= 4:
                    pe.wait_ge(oT_split, v - 3)
                for t in range(TB):
                    ins = tr(bank[v % 4][:, t * P:(t + 1) * P], o[:, t, v * P:(v + 1) * P], ident[:])
                ins.then_inc(oT_done, 1)
            for d in range(KC):
                b = bank[4 * (d % 2):4 * (d % 2) + 4]
                if d == 0:
                    pe.wait_ge(oT_split, KC)
                if d >= 2:
                    pe.wait_ge(merged, d - 1)
                columns(b[0][:], x_hi, x_lo)
                columns(b[1][:], x_hi, x_lo)
                columns(b[2][:], o_hi, o_lo)
                columns(b[3][:], f_hi, f_lo, 4)
            pe.wait_ge(m_split, KC)
            rows(bank[0:4], m_hi, m_lo)
            rows(bank[4:8], m_hi, m_lo)
            for k in range(KC):
                if k == 0:
                    pe.wait_ge(x1_ready, TB)
                if k >= 4:
                    pe.wait_ge(x1T_split, k - 3)
                for t in range(TB):
                    ins = tr(bank[k % 4][:, t * P:(t + 1) * P], x1[:, t, k * P:(k + 1) * P], ident[:])
                ins.then_inc(x1T_done, 1)
            pe.wait_ge(x1T_split, KC)
            for c in range(HP):
                if c >= 4:
                    pe.wait_ge(q_evac, c - 3)
                columns(bank[4 + c % 4][:], x_hi, x_lo)
            pe.wait_ge(q_evac, HP)
            pe.wait_ge(keys_in, 16)

            def score_tile(n, slot, b, split, free):
                pe.wait_ge(split_done, split)
                pe.wait_ge(gelu_done, free)
                for c in range(KC):
                    w = slice(c * P, (c + 1) * P)
                    ins = mm3(bank[b][:], w_hi[:, slot, w], w_lo[:, slot, w], x_hi[:, c, :], x_lo[:, c, :],
                              c == 0, c == KC - 1)
                ins.then_inc(quarter_used, 1)

            tile = [0]

            def score_tiles(count):
                for _ in range(count):
                    n = first_expert + tile[0]
                    score_tile(n, n % RING, tile[0] % 4, n + 1, tile[0] + 1)
                    tile[0] += 1

            def key_scores(t):
                if t >= 2:
                    pe.wait_ge(picks_evac, t - 1)
                for g in range(4):
                    if t >= 1:
                        pe.wait_ge(sc_evac, 4 * (t - 1) + g + 1)
                    for j in range(4):
                        hp = 4 * g + j
                        ins = mm(bank[4 + g][:, j * P:(j + 1) * P], qT[:, hp, t * P:(t + 1) * P], keys[:, hp, :],
                                 start=True, stop=True)
                    ins.then_inc(sc_done, 1)

            pe.sem_inc(gelu_done, 4)
            key_scores(0)
            for t in range(TB):
                score_tiles(TOPK_TILES // 2)
                if t + 1 < TB:
                    key_scores(t + 1)
                score_tiles(TOPK_TILES // 2)
                pe.wait_ge(picks_ready, t + 1)
                pe.wait_ge(sc_evac, 4 * min(t + 2, TB))
                for a in range(3):
                    ins = tr(bank[4][:, a * P:(a + 1) * P], ijg[:, a, :], ident[:])
                ins.then_inc(picks_turned, 1)

            pe.wait_ge(picks_evac, TB)
            pe.sem_inc(gm_done, 2)
            with pe.Fori(0, NGB // 2) as i:
                for k in range(GATE_TILES):
                    score_tile(None, (UNIT + k) % RING, k % 4, i * RING + (first_gate + k + 1),
                               i * RING + (TOPK_TILES * TB + k + 1))
                    for g in (2 * k, 2 * k + 1):
                        pe.wait_ge(oh_ready, i * 16 + (g + 1))
                        pe.wait_ge(gm_evac, i * 16 + (g + 1))
                        for j in range(4):
                            dst = bank[4 + g % 4][:, j * P:(j + 1) * P]
                            mm(dst, oh_j[:, g % 2, j, :], oh_lo[:, g % 2, j, :], start=True, stop=False)
                            ins = mm(dst, oh_j[:, g % 2, j, :], oh_hi[:, g % 2, j, :], start=False, stop=True)
                        ins.then_inc(gm_done, 1)

            def combine(u, n, slot, w):
                pe.wait_ge(wt_done, u * UNIT + UNIT)
                pe.wait_ge(split_done, n + UNIT)
                for m in range(8):
                    t, half = divmod(m, 2)
                    pe.wait_ge(acc_done, u * 8 + (m + 1))
                    for k in range(UNIT):
                        r, c = slice(t * P, (t + 1) * P), slice(half * 512, half * 512 + 512)
                        ins = mm3(bank[4 + m % 4][:], wt_hi[:, w, k, r], wt_lo[:, w, k, r],
                                  w_hi[:, slot + k, c], w_lo[:, slot + k, c], k == 0, k == UNIT - 1)
                    ins.then_inc(ffn_done, 1)

            pe.wait_ge(gm_evac, NGB * 8 + 4)
            pe.sem_inc(ffn_done, 8)
            with pe.Fori(0, mixed_units // 2) as i:
                for j in range(2):
                    for k in range(UNIT):
                        score_tile(None, UNIT + k, k, i * (2 * RING) + (first_mixed + RING * j + k + 1),
                                   i * (2 * UNIT) + (ahead_tiles + UNIT * j + k + 1))
                    combine(i * 2 + j, i * (2 * RING) + (first_mixed + RING * j + UNIT), 0, j)
            with pe.Fori(0, (NUNIT - mixed_units) // 2) as i:
                for j in range(2):
                    combine(i * 2 + (mixed_units + j), i * RING + (first_tail + UNIT * j), UNIT * (1 - j), j)

        @block.scalar
        def _(sc):
            act_f = nc.scalar.activation
            steps = [0]

            def step(ins):
                steps[0] += 1
                ins.then_inc(act_step, 1)
                sc.wait_ge(act_step, steps[0])

            next_hi = [0]

            def round_quarter(n, slot, width, land, free):
                sc.wait_ge(landed[slot % STAGE], land)
                if free is not None:
                    sc.wait_ge(quarter_used, free)
                act_f(w_hi[:, slot, 0:width], stage[:, slot % STAGE, 0:width], ACT.Copy).then_inc(hi_done, 1)

            def ahead(n):
                for m in range(next_hi[0], n + 1):
                    fox = first_merge <= m < first_wout and (m - first_merge) % 4 == 3
                    round_quarter(m, m % RING, 512 if fox else QW, 16 * (m // STAGE + 1),
                                  m - RING + 1 if m >= RING else None)
                next_hi[0] = max(next_hi[0], n + 1)

            sc.dma_start(small_sb[:], small_w).then_inc(small_in, 16)
            sc.dma_start(gate_up_sb[0:GRANK, :], gate_up).then_inc(gate_up_in, 16)
            sc.dma_start(gate_up_sb[GRANK:GRANK + 1, :], gate_bias).then_inc(gate_up_in, 16)
            sc.dma_start(f_bias, fox_f_bias.rearrange("a h -> h a")).then_inc(bias_in, 16)
            sc.wait_ge(xt_in, 16)
            for k in range(KC):
                act_f(x_hi[:, k, :], xT_raw[:, k, :], ACT.Copy).then_inc(xt_hi, 1)
            ahead(3)
            sc.wait_ge(const_made, 1)
            sc.wait_ge(small_done, 2)
            act_f(glrT[0:GRANK, :], bank[6][0:GRANK, :], ACT.Copy).then_inc(glr_ready, 1)
            sc.wait_ge(bias_in, 16)
            step(act_f(logf[:], bank[7][0:FH, :], ACT.Identity, bias=f_bias))
            step(act_f(logf2[:], logf[:], ACT.Abs))
            step(act_f(logf2[:], logf2[:], ACT.Exp, scale=-1.0))
            act_f(logf2[:], logf2[:], ACT.Ln, bias=1.0).then_inc(ff_ready, 1)

            for u, name in enumerate(PT_UNITS):
                for r in range(4):
                    b = bank[4 * (u % 2) + r]
                    seen = 4 * sum(x not in AUX for x in PT_UNITS[:u])
                    ahead(seen + 5 + (r if name in ("fq", "fk", "gq") else 0 if name in AUX else 3 if r == 0 else 3))
                    wait_product(sc, name, r)
                    if name == "fq":
                        if r == 0:
                            sc.wait_ge(xt_split, KC)
                        act_f(fqT[:, r, :], b[:], ACT.Copy, scale=FD ** -0.5).then_inc(proj_evac, 1)
                    elif name == "fk":
                        act_f(fkT[:, r, :], b[:], ACT.Copy).then_inc(proj_evac, 1)
                    elif name == "fv":
                        act_f(fv[:, r, :], b[:], ACT.Copy).then_inc(proj_evac, 1)
                    elif name == "gk":
                        act_f(kdec[:, r, :], b[:], ACT.Copy).then_inc(proj_evac, 1)
                    elif name == "gq":
                        act_f(gqT[:, r, :], b[:], ACT.Copy, scale=GK ** -0.5).then_inc(proj_evac, 1)
                    elif name in ("gv0", "gv1"):
                        if r == 0 and name == "gv0":
                            sc.wait_ge(xt_split, KC)
                        c = 512 * (name == "gv1")
                        act_f(gv[:, r, c:c + 512], b[:], ACT.Copy).then_inc(proj_evac, 1)
                    elif name == "z":
                        if r == 0:
                            sc.wait_ge(cum_ready, 1)
                        if r >= 2:
                            sc.wait_ge(la_ready, r - 1)
                        step(act_f(la[:, r, :], b[:], ACT.Copy))
                        step(act_f(tmp[:, r % 2, :], la[:, r, :], ACT.Abs))
                        step(act_f(tmp[:, r % 2, :], tmp[:, r % 2, :], ACT.Exp, scale=-1.0))
                        act_f(tmp[:, r % 2, :], tmp[:, r % 2, :], ACT.Ln, bias=1.0).then_inc(proj_evac, 1)
                    elif name == "sfx":
                        if r == 0:
                            sc.wait_ge(la_ready, TB)
                        if r >= 2:
                            sc.wait_ge(kdec_ready, r - 1)
                        act_f(tmp[:, r % 2, :], b[:], ACT.Exp, scale=1.0 / GATE_TEMP).then_inc(proj_evac, 1)
                    elif name == "tot":
                        act_f(etot[:, r, :], b[:, 0:NCH], ACT.Exp, scale=1.0 / GATE_TEMP).then_inc(proj_evac, 1)

            NS = FH * TB
            ahead(first_merge - 8 + 5)
            sc.wait_ge(kdec_ready, TB)
            for i in range(NS + 4):
                if i < NS:
                    w = (i % TB + 1) * P
                    sc.wait_ge(fox_max, i + 1)
                    if i >= 3:
                        sc.wait_ge(fox_turned, i - 2)
                    act_f(probs[:, i % 3, 0:w], bank[i % 3][:, 0:w], ACT.Exp, bias=negmax[:, i:i + 1],
                          accum_out=psums[:, i:i + 1]).then_inc(fox_exp, 1)
                if 2 <= i < NS + 2:
                    s = i - 2
                    w = (s % TB + 1) * P
                    sc.wait_ge(fox_turned, s + 1)
                    if s >= 2:
                        sc.wait_ge(fox_pv, s - 1)
                    act_f(pT[:, s % 2, 0:w], bank[3 + s % 2][:, 0:w], ACT.Copy).then_inc(fox_pT, 1)
                if i >= 4 and (i - 4) % 8 == 7:
                    c = (i - 4) // 8
                    sc.wait_ge(fox_pv, i - 3)
                    act_f(f_hi[:, c, :], bank[5 + c % 2][:], ACT.Copy).then_inc(fox_hi, 1)

            sc.dma_start(gla_gain_sb[:], gla_gain.broadcast_to([P, D])).then_inc(gla_gain_in, 16)
            for t in range(TB):
                sc.wait_ge(o_read, 8 * (t + 1))
                if t >= 1:
                    sc.wait_ge(o_evac, t)
                for half in range(2):
                    b = bank[4 + 2 * (t % 2) + half]
                    act_f(o[:, t, half * 512:half * 512 + 512], b[:], ACT.Copy)
                    for j in range(2):
                        ins = act_f(tmp[:, half, j * GV:(j + 1) * GV], b[:, j * GV:(j + 1) * GV], ACT.Square,
                                    accum_out=ss[:, 4 * t + 2 * half + j:4 * t + 2 * half + j + 1])
                ins.then_inc(o_evac, 1)
            sc.wait_ge(o_evac, TB)
            act_f(rs, ss, ACT.Sqrt, bias=eps_col, scale=1.0 / GV).then_inc(rms_sqrt, 1)
            for r in range(8):
                ahead(first_merge - 8 + 8 + 4 * (r // 4))
                wait_product(sc, f"gg{r // 4}", r % 4)
                if r >= 2:
                    sc.wait_ge(o_gated, r - 1)
                act_f(tmp[:, r % 2, :], bank[r][:], ACT.Silu).then_inc(silu_ready, 1)
            for v in range(KC):
                sc.wait_ge(oT_done, v + 1)
                act_f(o_hi[:, v, :], bank[v % 4][:], ACT.Copy).then_inc(oT_hi, 1)
            for d in range(KC):
                b = bank[4 * (d % 2):4 * (d % 2) + 4]
                if d >= 2:
                    sc.wait_ge(merged, d - 1)
                ahead(first_merge + 4 * d + 5)
                sc.wait_ge(quarter_used, first_merge + 4 * d + 1)
                act_f(sig_a[:, d % 2, :], b[0][:], ACT.Sigmoid).then_inc(sig_ready, 1)
                ahead(first_merge + 4 * d + 7)
                sc.wait_ge(quarter_used, first_merge + 4 * d + 2)
                act_f(sig_b[:, d % 2, :], b[1][:], ACT.Sigmoid).then_inc(sig_ready, 1)
            sc.wait_ge(quarter_used, first_wout)
            sc.dma_start(x1[:], x.rearrange("(t p) d -> p t d", p=P)).then_inc(x_in, 16)
            for d in range(KC):
                sc.wait_ge(merged, d + 1)
                act_f(m_hi[:, d, :], mT[:, d, :], ACT.Copy).then_inc(m_hi_done, 1)
            ahead(first_query + 2)
            sc.dma_start(ln_g1[:], ln1_gain.broadcast_to([P, D])).then_inc(gain_in, 16)
            sc.dma_start(ln_b1[:], ln1_bias.broadcast_to([P, D])).then_inc(gain_in, 16)
            sc.wait_ge(ln_var, 1)
            act_f(sd, mv[:, :, 1], ACT.Sqrt, bias=eps_col).then_inc(ln_sqrt, 1)
            sc.wait_ge(quarter_used, first_query)
            sc.dma_start(keys[:], keysT).then_inc(keys_in, 16)
            for t in range(TB):
                sc.wait_ge(x1_ready, t + 1)
                act_f(acc[:, t, :], x1[:, t, :], ACT.Copy, scale=ALPHA).then_inc(acc_ready, 1)
            for k in range(KC):
                sc.wait_ge(x1T_done, k + 1)
                act_f(x_hi[:, k, :], bank[k % 4][:], ACT.Copy).then_inc(x1T_hi, 1)
            for c in range(HP):
                ahead(first_query + c + 5)
                sc.wait_ge(quarter_used, first_query + c + 1)
                act_f(qT[:, c, :], bank[4 + c % 4][:], ACT.Copy).then_inc(q_evac, 1)

            def gelu_out(tile, parity, b, n_used, turn):
                sc.wait_ge(quarter_used, n_used)
                if turn is not None:
                    sc.wait_ge(act_written[parity], turn)
                act_f(act_out[parity][:], bank[b][:], ACT.Gelu).then_inc(gelu_done, 1)

            def store_tile(tile, parity, dst):
                sc.wait_ge(gelu_done, tile + 5)
                sc.dma_start(act_out_view(dst), act_out[parity][:]).then_inc(act_written[parity], 16)

            def act_out_view(dst):
                return dst

            tile = [0]

            def gelus(count):
                for _ in range(count):
                    t = tile[0]
                    gelu_out(t, t % 2, t % 4, first_expert + t + 1, 16 * (t // 2) if t >= 2 else None)
                    ahead(first_expert + t + 4)
                    store_tile(t, t % 2, act_dram[t // UNIT, :, t % UNIT, :])
                    tile[0] += 1

            def evac_scores(t):
                if t >= 1:
                    sc.wait_ge(sc_used, t)
                for g in range(4):
                    sc.wait_ge(sc_done, 4 * t + g + 1)
                    act_f(score[:, 4 * g:4 * g + 4, :],
                          bank[4 + g][:].rearrange("p (a n) -> p a n", a=4), ACT.Copy).then_inc(sc_evac, 1)

            sc.wait_ge(acc_ready, TB)
            evac_scores(0)
            for t in range(TB):
                gelus(TOPK_TILES // 2)
                if t + 1 < TB:
                    evac_scores(t + 1)
                gelus(TOPK_TILES // 2 - 1)
                sc.wait_ge(best_ready, t + 1)
                act_f(ijg[:, 2, :], ijg[:, 2, :], ACT.Exp).then_inc(gate_exp, 1)
                gelus(1)
                sc.wait_ge(picks_turned, t + 1)
                act_f(picks[:, :, t * P:(t + 1) * P],
                      bank[4][:, 0:3 * P].rearrange("p (a t) -> p a t", a=3), ACT.Copy).then_inc(picks_evac, 1)

            sc.sem_inc(gm_evac, 4)

            def gate_batches(i, first):
                for k in range(GATE_TILES):
                    half = k // 4
                    if not first and k % 4 == 0:
                        sc.wait_ge(gm_written[half], i * 16)
                    for g in (2 * k, 2 * k + 1):
                        sc.wait_ge(gm_done, i * 16 + (g + 3))
                        t0 = 4 * (g % 8)
                        act_f(gstage[half][:, :, t0:t0 + 4],
                              bank[4 + g % 4][:].rearrange("p (t i) -> p i t", t=4), ACT.Copy).then_inc(gm_evac, 1)
                    t = i * GATE_TILES + (TOPK_TILES * TB + k)
                    n = i * RING + (first_gate + k)
                    gelu_out(t, k % 2, k % 4, n + 1, i * 64 + 16 * ((TOPK_TILES * TB + k) // 2))
                    round_quarter(n + 4, k, QW, i * 32 + 16 * ((first_gate + k + 4) // STAGE + 1), n - 3)
                    u = i * 2 + (TOPK_TILES * TB // UNIT + k // UNIT)
                    store_tile(t, k % 2, act_dram[bass.ds(u, 1), :, k % UNIT, :].rearrange("u p c -> p (u c)"))
                    if k % 4 == 3:
                        sc.wait_ge(gm_evac, i * 16 + (4 + 8 * (half + 1)))
                        sc.dma_start(gate_dram[:, :, bass.ds(i * 2 + half, 1), :].rearrange("u p b c -> p u (b c)"),
                                     gstage[half][:, :, :].rearrange("p (u c) t -> p u (c t)", c=UNIT))\
                            .then_inc(gm_written[half], 16)

            gate_batches(0, True)
            with sc.Fori(1, NGB // 2) as i:
                gate_batches(i, False)

            def load_unit(u):
                for parity in range(2):
                    sc.wait_ge(act_written[parity], u * 32 + 32)
                sc.dma_start(gates[:].rearrange("p b c t -> p (b c t)"),
                             gate_dram[bass.ds(u, 1), :, :, :].rearrange("u p b c -> p (u b c)")).then_inc(gates_in, 16)
                sc.dma_start(act[:].rearrange("p c t -> p (c t)"),
                             act_dram[bass.ds(u, 1), :, :, :].rearrange("u p c t -> p (u c t)")).then_inc(act_in, 16)

            for half in range(2):
                sc.wait_ge(gm_written[half], 16 * NGB // 2)
            load_unit(0)
            sc.dma_start(ln_g2[:], ln2_gain.broadcast_to([P, D])).then_inc(ln2_in, 16)
            sc.dma_start(ln_b2[:], ln2_bias.broadcast_to([P, D])).then_inc(ln2_in, 16)

            def round_values(n_land, slot, used):
                sc.wait_ge(ffn_done, used)
                for k in range(UNIT):
                    round_quarter(None, slot + k, QW, n_land, None)

            with sc.Fori(0, mixed_units) as u:
                sc.wait_ge(wt_done, u * UNIT + UNIT)
                load_unit(u + 1)
                sc.wait_ge(quarter_used, u * UNIT + (first_mixed))
                round_values(u * 32 + 16 * ((first_mixed + UNIT) // STAGE + 1), 0, u * 8 + 8)
                for k in range(UNIT):
                    t = u * UNIT + (ahead_tiles + k)
                    gelu_out(t, k % 2, k, t + (first_expert + 1), u * 32 + 16 * ((ahead_tiles + k) // 2))
                    round_quarter(None, UNIT + k, QW, u * 32 + 16 * ((first_mixed + RING + k) // STAGE + 1),
                                  t + (first_expert + 1))
                    store_tile(t, k % 2, act_dram[bass.ds(u + ahead_units, 1), :, k, :].rearrange("u p c -> p (u c)"))

            def tail_unit(u, j, land):
                sc.wait_ge(wt_done, u * UNIT + UNIT)
                load_unit(u + 1)
                round_values(land, UNIT * j, u * 8 + 8)

            with sc.Fori(0, (NUNIT - mixed_units) // 2 - 1) as i:
                for j in range(2):
                    tail_unit(i * 2 + (mixed_units + j), j, i * 32 + 16 * ((first_tail + UNIT * (j + 1)) // STAGE + 1))
            tail_unit(NUNIT - 2, 0, 16 * ((first_tail + UNIT * (NUNIT - mixed_units - 1)) // STAGE + 1))
            sc.wait_ge(ln2_var, 1)
            act_f(sd, mv[:, :, 1], ACT.Sqrt, bias=eps_col).then_inc(ln2_sqrt, 1)

        @block.vector
        def _(dve):
            v = nc.vector
            steps = [0]

            def step(ins):
                steps[0] += 1
                ins.then_inc(dve_step, 1)
                dve.wait_ge(dve_step, steps[0])

            for k in range(KC):
                dve.wait_ge(xt_hi, k + 1)
                v.tensor_tensor(x_lo[:, k, :], xT_raw[:, k, :], x_hi[:, k, :], ALU.subtract).then_inc(xt_split, 1)
            step(v.memset(zero_row[:], 0.0))
            dve.wait_ge(ff_ready, 1)
            step(v.scalar_tensor_tensor(out=logf[:], in0=logf[:], scalar=0.0, in1=logf2[:], op0=ALU.min, op1=ALU.subtract))
            v.tensor_tensor_scan(cum[:], logf[:], zero_row[:], 0.0, ALU.add, ALU.add).then_inc(cum_ready, 1)
            for r in range(TB):
                dve.wait_ge(proj_evac, 8 + r + 1)
                v.scalar_tensor_tensor(out=la[:, r, :], in0=la[:, r, :], scalar=0.0, in1=tmp[:, r % 2, :],
                                       op0=ALU.min, op1=ALU.subtract).then_inc(la_ready, 1)
            for r in range(TB):
                dve.wait_ge(proj_evac, 20 + r + 1)
                v.tensor_tensor(kdec[:, r, :], kdec[:, r, :], tmp[:, r % 2, :], ALU.mult).then_inc(kdec_ready, 1)
            NS = FH * TB
            for i in range(NS + 4):
                if i < NS:
                    w = (i % TB + 1) * P
                    dve.wait_ge(fox_logits, i + 1)
                    v.tensor_reduce(negmax[:, i:i + 1], bank[i % 3][:, 0:w], AX.X, ALU.max, negate=True).then_inc(fox_max, 1)
                if 1 <= i < NS + 1:
                    s = i - 1
                    w = (s % TB + 1) * P
                    dve.wait_ge(fox_exp, s + 1)
                    step(v.reciprocal(recips[:, s:s + 1], psums[:, s:s + 1]))
                    v.tensor_scalar(probs[:, s % 3, 0:w], probs[:, s % 3, 0:w], recips[:, s:s + 1], None,
                                    ALU.mult).then_inc(fox_norm, 1)
                if i >= 4 and (i - 4) % 8 == 7:
                    c = (i - 4) // 8
                    dve.wait_ge(fox_hi, c + 1)
                    v.tensor_tensor(f_lo[:, c, :], bank[5 + c % 2][:], f_hi[:, c, :], ALU.subtract).then_inc(fox_split, 1)
            for c in range(NCH):
                for h in range(GH):
                    dve.wait_ge(kv_done, 4 * c + h + 1)
                    if c >= 2:
                        dve.wait_ge(o_read, 4 * (c - 2) + h + 1)
                    if c == 0:
                        v.tensor_copy(state[:, 0, h, :], bank[h][:, 0:GV]).then_inc(state_done, 1)
                    else:
                        dve.wait_ge(state_done, 4 * (c - 1) + h + 1)
                        v.scalar_tensor_tensor(out=state[:, c % 2, h, :], in0=state[:, 1 - c % 2, h, :],
                                               scalar=etot[:, h, c:c + 1], in1=bank[h][:, 0:GV],
                                               op0=ALU.mult, op1=ALU.add).then_inc(state_done, 1)
            dve.wait_ge(rms_sqrt, 1)
            step(v.reciprocal(rs, rs))
            dve.wait_ge(gla_gain_in, 16)
            for t in range(TB):
                for h in range(GH):
                    c = slice(h * GV, (h + 1) * GV)
                    ins = v.scalar_tensor_tensor(out=o[:, t, c], in0=o[:, t, c], scalar=rs[:, 4 * t + h:4 * t + h + 1],
                                                 in1=gla_gain_sb[:, c], op0=ALU.mult, op1=ALU.mult)
            step(ins)
            for r in range(8):
                dve.wait_ge(silu_ready, r + 1)
                half, t = divmod(r, TB)
                c = slice(half * 512, half * 512 + 512)
                v.tensor_tensor(o[:, t, c], o[:, t, c], tmp[:, r % 2, :], ALU.mult).then_inc(o_gated, 1)
            for k in range(KC):
                dve.wait_ge(oT_hi, k + 1)
                v.tensor_tensor(o_lo[:, k, :], bank[k % 4][:], o_hi[:, k, :], ALU.subtract).then_inc(oT_split, 1)
            for d in range(KC):
                b = bank[4 * (d % 2):4 * (d % 2) + 4]
                dve.wait_ge(sig_ready, 2 * d + 2)
                dve.wait_ge(quarter_used, first_merge + 4 * d + 4)
                v.tensor_tensor(sig_a[:, d % 2, :], sig_a[:, d % 2, :], b[3][:], ALU.mult)
                step(v.tensor_tensor(sig_b[:, d % 2, :], sig_b[:, d % 2, :], b[2][:], ALU.mult))
                v.tensor_tensor(mT[:, d, :], sig_a[:, d % 2, :], sig_b[:, d % 2, :], ALU.add).then_inc(merged, 1)
            for d in range(KC):
                dve.wait_ge(m_hi_done, d + 1)
                v.tensor_tensor(m_lo[:, d, :], mT[:, d, :], m_hi[:, d, :], ALU.subtract).then_inc(m_split, 1)
            dve.wait_ge(x_in, 16)
            for r in range(8):
                half, t = divmod(r, TB)
                dve.wait_ge(quarter_used, first_wout + 4 * (half + 1))
                c = slice(half * 512, half * 512 + 512)
                ins = v.scalar_tensor_tensor(out=x1[:, t, c], in0=x1[:, t, c], scalar=ALPHA, in1=bank[r][:],
                                             op0=ALU.mult, op1=ALU.add)
            step(ins)

            def norm_stats(src):
                for t in range(TB):
                    for half in range(2):
                        ins = v.bn_stats(stats[:, 12 * t + 6 * half:12 * t + 6 * half + 6], src[:, t, half * 512:half * 512 + 512])
                step(ins)
                for t in range(TB):
                    ins = v.bn_aggr(mv[:, t, :], stats[:, 12 * t:12 * t + 12])
                return ins

            def norm_apply(src, gain, bias, done):
                step(v.reciprocal(sd, sd))
                for t in range(TB):
                    step(v.tensor_scalar(src[:, t, :], src[:, t, :], mv[:, t, 0:1], sd[:, t:t + 1], ALU.subtract, ALU.mult))
                    step(v.tensor_tensor(src[:, t, :], src[:, t, :], gain[:], ALU.mult))
                    v.tensor_tensor(src[:, t, :], src[:, t, :], bias[:], ALU.add).then_inc(done, 1)

            norm_stats(x1).then_inc(ln_var, 1)
            dve.wait_ge(ln_sqrt, 1)
            dve.wait_ge(gain_in, 32)
            norm_apply(x1, ln_g1, ln_b1, x1_ready)
            for k in range(KC):
                dve.wait_ge(x1T_hi, k + 1)
                v.tensor_tensor(x_lo[:, k, :], bank[k % 4][:], x_hi[:, k, :], ALU.subtract).then_inc(x1T_split, 1)

            square = [P, PH, TOPK, TOPK]
            dve.wait_ge(acc_ready, TB)
            v.tensor_copy(iota_o[:], iota_n[:, 0:TOPK])
            for t in range(TB):
                dve.wait_ge(sc_evac, 4 * t + 4)

                def top16(vals, idx, src, rows_n):
                    for a in range(rows_n):
                        ins = v.max(vals[:, a, 0:8], src[:, a, :])
                    step(ins)
                    for a in range(rows_n):
                        ins = v.max_index(idx[:, a, 0:8], vals[:, a, 0:8], src[:, a, :])
                    step(ins)
                    for a in range(rows_n):
                        ins = v.match_replace(src[:, a, :], vals[:, a, 0:8], src[:, a, :], NEG_REPLACE)
                    step(ins)
                    for a in range(rows_n):
                        ins = v.max(vals[:, a, 8:16], src[:, a, :])
                    step(ins)
                    for a in range(rows_n):
                        ins = v.max_index(idx[:, a, 8:16], vals[:, a, 8:16], src[:, a, :])
                    return ins

                top16(top_v, top_i, score, HP).then_inc(sc_used, 1)
                dve.wait_ge(sc_used, t + 1)
                v.tensor_copy(top_if[:], top_i[:])
                tv = top_v[:].rearrange("p (h s) k -> p h s k", s=2)
                step(v.tensor_tensor(
                    cand[:].rearrange("p h (a b) -> p h a b", a=TOPK),
                    tv[:, :, 0, :].unsqueeze(3).broadcast_to(square), tv[:, :, 1, :].unsqueeze(2).broadcast_to(square), ALU.add))
                step(top16(best, pos, cand, PH))
                if t >= 1:
                    dve.wait_ge(picks_turned, t)
                v.tensor_tensor(ijg[:, 2, :].rearrange("p (h k) -> p h k", h=PH), best[:],
                                best[:, :, 0:1].broadcast_to([P, PH, TOPK]), ALU.subtract).then_inc(best_ready, 1)
                v.tensor_scalar(pos_i[:, 0, :, :], pos[:], 4, None, ALU.logical_shift_right)
                step(v.tensor_scalar(pos_i[:, 1, :, :], pos[:], TOPK - 1, None, ALU.bitwise_and))
                step(v.tensor_copy(pos_f[:], pos_i[:]))
                ti = top_if[:].rearrange("p (h s) k -> p h s k", s=2)
                eq = cand[:].rearrange("p h (k o) -> p h k o", o=TOPK)
                for a in range(2):
                    step(v.tensor_tensor(eq, pos_f[:, a, :, :].unsqueeze(3).broadcast_to(square),
                                         iota_o[:].unsqueeze(1).unsqueeze(1).broadcast_to(square), ALU.is_equal))
                    step(v.tensor_tensor(eq, eq, ti[:, :, a, :].unsqueeze(2).broadcast_to(square), ALU.mult))
                    step(v.tensor_reduce(ijg[:, a, :].rearrange("p (h k) -> p h k", h=PH), eq, AX.X, ALU.add))
                dve.wait_ge(gate_exp, t + 1)
                gx = ijg[:, 2, :].rearrange("p (h k) -> p h k", h=PH)
                step(v.tensor_reduce(gsum, gx, AX.X, ALU.add))
                step(v.reciprocal(grec, gsum))
                v.tensor_tensor(gx, gx, grec.unsqueeze(2).broadcast_to([P, PH, TOPK]), ALU.mult).then_inc(picks_ready, 1)

            dve.wait_ge(picks_evac, TB)
            v.tensor_copy(gate_parts[:, 0, :], picks[:, 2, :]).then_inc(gate_split, 1)
            dve.wait_ge(gate_split, 1)
            v.tensor_tensor(gate_parts[:, 1, :], picks[:, 2, :], gate_parts[:, 0, :], ALU.subtract).then_inc(gate_split, 1)
            dve.wait_ge(gate_split, 2)
            with dve.Fori(0, NGB // 2) as i:
                for g in range(16):
                    dve.wait_ge(gm_done, i * 16 + (g + 1))
                    v.tensor_tensor(oh_j[:, g % 2, :, :], iota_n[:].unsqueeze(1).broadcast_to([P, 4, NKEY]),
                                    picks[:, 1, bass.ds(i * 64 + 4 * g, 4)].unsqueeze(2).broadcast_to([P, 4, NKEY]),
                                    ALU.is_equal)
                    for j in range(4):
                        tok = i * 64 + (4 * g + j)
                        for part, oh in ((0, oh_hi), (1, oh_lo)):
                            ins = v.tensor_scalar(oh[:, g % 2, j, :], iota_n[:], picks[:, 0, bass.ds(tok, 1)],
                                                  gate_parts[:, part, bass.ds(tok, 1)].bitcast(F32), ALU.is_equal, ALU.mult)
                    ins.then_inc(oh_ready, 1)

            def weigh(u, k, w):
                n = u * UNIT + (k + 1)
                if k == 0:
                    dve.wait_ge(gates_in, u * 16 + 16)
                    dve.wait_ge(act_in, u * 16 + 16)
                a = act[:, k, :]
                v.tensor_tensor(a.rearrange("p (b t) -> p b t", b=NGB), a.rearrange("p (b t) -> p b t", b=NGB),
                                gates[:, :, k, :], ALU.mult).then_inc(wt_mul, 1)
                dve.wait_ge(wt_mul, n)
                v.tensor_copy(wt_hi[:, w, k, :], a).then_inc(wt_hi_done, 1)
                dve.wait_ge(wt_hi_done, n)
                v.tensor_tensor(wt_lo[:, w, k, :], a, wt_hi[:, w, k, :], ALU.subtract).then_inc(wt_done, 1)

            def add_out(u, m):
                t, half = divmod(m, 2)
                c = slice(half * 512, half * 512 + 512)
                dve.wait_ge(acc_done, u * 8 + (m + 1))
                dve.wait_ge(ffn_done, u * 8 + (m + 9))
                v.tensor_tensor(acc[:, t, c], acc[:, t, c], bank[4 + m % 4][:], ALU.add).then_inc(acc_done, 1)

            def unit_out(u, w):
                for m in range(8):
                    add_out(u, m)
                    if w is not None and 2 <= m < 2 + UNIT:
                        if m == 2:
                            dve.wait_ge(ffn_done, u * 8 + 8)
                        weigh(u + 1, m - 2, w)

            for k in range(UNIT):
                weigh(0, k, 0)
            dve.sem_inc(acc_done, 4)
            with dve.Fori(0, NUNIT // 2 - 1) as i:
                unit_out(i * 2, 1)
                unit_out(i * 2 + 1, 0)
            unit_out(NUNIT - 2, 1)
            unit_out(NUNIT - 1, None)
            dve.wait_ge(acc_done, 8 * NUNIT + 4)
            norm_stats(acc).then_inc(ln2_var, 1)
            dve.wait_ge(ln2_sqrt, 1)
            dve.wait_ge(ln2_in, 32)
            norm_apply(acc, ln_g2, ln_b2, y_ready)


def kernel(**inputs):
    import numpy as np
    import concourse.bacc as bacc
    from concourse.bass_utils import run_bass_kernel_spmd

    def of(name):
        return np.ascontiguousarray(inputs[name])[0]

    x = of("x")
    w_in = of("w_in")
    widths = [512, 512, 512, FH, GH * GK, GH * GK, D, D, GRANK, D, D]
    at = [sum(widths[:i]) for i in range(len(widths))]
    fq, fk, fv, ff, gq, gk, gv, gg, glr, mga, mgb = [w_in[:, a:a + n] for a, n in zip(at, widths)]

    def columns(w, c):
        k = w.shape[0] // P
        return w[:, c * P:(c + 1) * P].reshape(k, P, P).transpose(1, 0, 2).reshape(P, k * P)

    def rows(w, half, q):
        return w[2 * P * q:2 * P * (q + 1), 512 * half:512 * half + 512].reshape(2, P, 512).transpose(1, 0, 2).reshape(P, 1024)

    quarters = [columns(fq, c) for c in range(4)] + [columns(fk, c) for c in range(4)]
    quarters += [rows(fv, 0, q) for q in range(4)] + [rows(gk, 0, q) for q in range(4)]
    quarters += [columns(gq, c) for c in range(4)]
    quarters += [rows(w, half, q) for w in (gv, gg) for half in range(2) for q in range(4)]
    w_gla, w_fox, w_out = of("w_out_gla"), of("w_out_fox"), of("w_out")
    for d in range(D // P):
        quarters += [columns(mga, d), columns(mgb, d), columns(w_gla, d)]
    quarters += [rows(w_out, half, q) for half in range(2) for q in range(4)]
    w_query = of("peer_w_query").reshape(D, HP * P)
    quarters += [columns(w_query, c) for c in range(HP)]

    arrays = {
        "xT": x.reshape(S, KC, P).transpose(2, 1, 0),
        "x": x.reshape(S, D),
        "mix_stream": np.stack(quarters),
        "fox_stream": np.stack([columns(w_fox, d) for d in range(D // P)]),
        "small_w": np.concatenate([ff, glr], axis=1).reshape(KC, P, FH + GRANK).transpose(1, 0, 2),
        "fox_f_bias": of("fox_f_bias")[None],
        "gate_up": of("gla_gate_up"),
        "gate_bias": of("gla_gate_bias")[None],
        "gla_gain": of("gla_norm_gain").reshape(1, D),
        "ln1_gain": of("ln1_gain")[None], "ln1_bias": of("ln1_bias")[None],
        "ln2_gain": of("ln2_gain")[None], "ln2_bias": of("ln2_bias")[None],
        "keysT": of("peer_sub_keys").reshape(HP, NKEY, P).transpose(2, 0, 1),
        "expert_uT": of("peer_expert_u").reshape(NKEY, NKEY, KC, P).transpose(0, 3, 2, 1).reshape(NKEY, P, D),
        "expert_v": of("peer_expert_v").reshape(NKEY, NKEY, D),
    }
    arrays = {k: np.ascontiguousarray(a) for k, a in arrays.items()}
    nc = bacc.Bacc("TRN2", target_bir_lowering=False, num_devices=1)
    args = {k: nc.dram_tensor(f"in_{k}", a.shape, mybir.dt.from_np(a.dtype), kind="ExternalInput").ap()
            for k, a in arrays.items()}
    out = nc.dram_tensor("out_0", (S, D), F32, kind="ExternalOutput").ap()
    build(nc, out=out, **args)
    r = run_bass_kernel_spmd(nc, [{f"in_{k}": a for k, a in arrays.items()}], core_ids=[0])
    return r.results[0]["out_0"].reshape(1, S, D)
```

```python
from contextlib import ExitStack

import concourse.bass as bass
from concourse import mybir

ALU = mybir.AluOpType
ACT = mybir.ActivationFunctionType
AX = mybir.AxisListType
F32 = mybir.dt.float32
F32R = mybir.dt.float32r
BF16 = mybir.dt.bfloat16
U32 = mybir.dt.uint32

P = 128
D = 1024
S = 512
KC = D // P
TB = S // P
CHUNK = 64
NCH = S // CHUNK
FH, FD = 8, 64
GH, GK, GV = 4, 128, 256
GRANK = 16
SMALL = 32 + GRANK
GATE_TEMP = 16.0
PH = 8
NKEY = 128
TOPK = 16
HP = 2 * PH
ALPHA = 2.0 ** 0.25
EPS = 1e-5
NEG = -1e30
NEG_REPLACE = -3.0e38

QW = 1024
RING = 8
STAGE = 4
UNIT = 4
NUNIT = NKEY // UNIT
GB = 32
GT = 4
TOPK_TILES = 10
GATE_TILES = 8
BRIDGE_TILES = 8
NGB = S // GB
KIB = 1024


def build(nc, xT, x, mix_stream, fox_stream, small_w, fox_f_bias, gate_up, gate_bias, gla_gain,
          ln1_gain, ln1_bias, ln2_gain, ln2_bias, keysT, expert_uT, expert_v, out):
    gate_dram = nc.dram_tensor("gate_scratch", [NUNIT, P, NGB, UNIT * GB], F32, kind="Internal").ap()
    act_dram = nc.dram_tensor("activation_scratch", [NUNIT, P, UNIT, S], F32, kind="Internal").ap()

    with ExitStack() as ctx:
        origin = (nc.sbuf_base + 127) // 128 * 128
        ctx.enter_context(nc.sbuf_tensor("arena", [P, (411 * KIB // 2 + 128) // 4], F32))

        def at(name, shape, dt, kib):
            return nc.alloc_sbuf_tensor_at(name, shape, dt, offset=origin + int(kib * KIB))

        stage = at("stage", [P, STAGE, QW], F32, 0)
        w_hi = at("w_hi", [P, RING, QW], F32R, 16)
        w_lo = at("w_lo", [P, RING, QW], F32R, 48)
        x_hi = at("x_hi", [P, KC, S], F32R, 80)
        x_lo = at("x_lo", [P, KC, S], F32R, 96)
        Q = 112
        small_sb = at("small_sb", [P, KC, SMALL], F32, Q + 0)
        glrT = at("glrT", [GRANK + 1, S], F32, Q + 1.5)
        gate_up_sb = at("gate_up_sb", [GRANK + 1, GH * GK], F32, Q + 3.5)
        xT_raw = at("xT_raw", [P, KC, S], F32, Q + 48)
        f_hi = at("f_hi", [P, 4, S], F32R, Q + 0)
        f_lo = at("f_lo", [P, 4, S], F32R, Q + 8)
        fqT = at("fqT", [P, 4, S], F32, Q + 16)
        fkT = at("fkT", [P, 4, S], F32, Q + 24)
        fv = at("fv", [P, TB, 512], F32, Q + 32)
        kdec = at("kdec", [P, TB, 512], F32, Q + 40)
        gv = at("gv", [P, TB, D], F32, Q + 48)
        gqT = at("gqT", [P, GH, S], F32, Q + 64)
        la = at("la", [P, TB, 512], F32, Q + 72)
        probs = at("probs", [P, 4, S], F32, Q + 72)
        state = at("state", [P, 2, GH, GV], F32, Q + 16)
        o = at("o", [P, TB, D], F32, Q + 24)
        o_hi = at("o_hi", [P, KC, S], F32R, Q + 40)
        o_lo = at("o_lo", [P, KC, S], F32R, Q + 56)
        sig_a = at("sig_a", [P, 2, S], F32, Q + 72)
        sig_b = at("sig_b", [P, 2, S], F32, Q + 76)
        m_hi = at("m_hi", [P, KC, S], F32R, Q + 16)
        m_lo_parts = [at("m_lo_a", [P, 4, S], F32R, Q + 32), at("m_lo_b", [P, 4, S], F32R, Q + 80 + 3)]
        x1 = at("x1", [P, TB, D], F32, Q + 0)
        acc = at("acc", [P, TB, D], F32, Q + 16)
        ln_g1 = at("ln_g1", [P, D], F32, Q + 72)
        ln_b1 = at("ln_b1", [P, D], F32, Q + 76)
        qT = at("qT", [P, HP, S], F32, Q + 32)
        keys = at("keys", [P, HP, NKEY], F32, Q + 64)
        score = at("score", [P, HP, NKEY], F32, Q + 72)
        cand = at("cand", [P, PH, TOPK * TOPK], F32, Q + 8)
        oh_j = at("oh_j", [P, 2, NKEY, GT], BF16, Q + 72)
        pick_keys = at("pick_keys", [P, 2, S], BF16, Q + 74)
        gate_parts = at("gate_parts", [P, 3, S], BF16, Q + 76)
        iota_g = at("iota_g", [P, NKEY, GT], BF16, Q + 79)
        oh_gate = at("oh_gate", [P, 2, 3, NKEY, GT], BF16, Q + 8)
        oh_i = at("oh_i", [P, 2, NKEY, GT], BF16, Q + 14)
        gstage = [at("gstage_a", [P, NKEY, GB], F32, Q + 32), at("gstage_b", [P, NKEY, GB], F32, Q + 48)]
        wt_hi = at("wt_hi", [P, 2, UNIT, S], F32R, Q + 32)
        wt_lo = at("wt_lo", [P, 2, UNIT, S], F32R, Q + 48)
        act = at("act", [P, UNIT, S], F32, Q + 64)
        gates = at("gates", [P, NGB, UNIT, GB], F32, Q + 72)
        ln_g2 = at("ln_g2", [P, D], F32, Q + 8)
        ln_b2 = at("ln_b2", [P, D], F32, Q + 12)
        E = Q + 80
        ident = at("ident", [P, P], F32, E)
        ident_b = at("ident_b", [P, P], BF16, E + 0.5)
        mask_b = at("mask_b", [P, P], BF16, E + 0.75)
        later = at("later", [P, P], F32, E + 1)
        iota_n = at("iota_n", [P, NKEY], F32, E + 1.5)
        tiny = at("tiny", [P, 256], F32, E + 2)
        head_sel_raw = at("head_sel_raw", [FH, FH, P], F32, Q + 8)
        head_sel = at("head_sel", [FH, FH, P], F32R, E + 3)
        cum_hi = at("cum_hi", [FH, S], F32R, Q + 6)
        cum_lo = at("cum_lo", [FH, S], F32R, Q + 14)
        gla_gain_sb = at("gla_gain_sb", [P, D], F32, E + 3)
        cum = at("cum", [FH, S], F32, E + 7)
        logf = at("logf", [FH, S], F32, E + 9)
        logf2 = at("logf2", [FH, S], F32, E + 11)
        zero_row = at("zero_row", [FH, S], F32, Q + 72)
        tmp = at("tmp", [P, 2, S], F32, E + 9)
        pT = at("pT", [P, 2, S], F32, E + 9)
        top_v = at("top_v", [P, HP, TOPK], F32, E + 3)
        top_i = at("top_i", [P, HP, TOPK], U32, E + 4)
        top_if = at("top_if", [P, HP, TOPK], F32, E + 5)
        best = at("best", [P, PH, TOPK], F32, E + 6)
        pos = at("pos", [P, PH, TOPK], U32, E + 6.5)
        pos_i = at("pos_i", [P, 2, PH, TOPK], U32, E + 7)
        pos_f = at("pos_f", [P, 2, PH, TOPK], F32, E + 8)
        ijg = at("ijg", [P, 3, P], F32, E + 9)
        picks = at("picks", [P, 3, S], F32, Q + 0)
        iota_o = at("iota_o", [P, TOPK], F32, E + 10.5)
        act_out = [at("act_out_a", [P, S], F32, Q + 6), at("act_out_b", [P, S], F32, E + 11)]

        stats = tiny[:, 0:48]
        ss = tiny[:, 48:64]
        rs = tiny[:, 64:80]
        etot = tiny[:, 80:112].rearrange("p (h c) -> p h c", h=GH)
        negmax = tiny[:, 112:144]
        psums = tiny[:, 144:176]
        recips = tiny[:, 176:208]
        chunk_ind = tiny[:, 208:210]
        eps_col = tiny[:, 210:211]
        mv = tiny[:, 212:220].rearrange("p (t s) -> p t s", t=TB)
        sd = tiny[:, 220:224]
        f_bias = tiny[0:FH, 224:225]
        gsum = tiny[:, 232:240]
        grec = tiny[:, 240:248]

        bank = [ctx.enter_context(nc.psum_tensor(f"bank{i}", [P, 512], F32)) for i in range(8)]
        fox_bank = [bank[0], bank[1], bank[2], bank[7]]

        def sem(name):
            return ctx.enter_context(nc.semaphore(name))

        landed = [sem(f"landed{i}") for i in range(STAGE)]
        hi_done, split_done, quarter_used = sem("hi_done"), sem("split_done"), sem("quarter_used")
        const_made, pool_step = sem("const_made"), sem("pool_step")
        xt_in = [sem(f"xt_in{i}") for i in range(4)]
        small_in, gate_up_in, bias_in, gla_gain_in, gain_in = sem("small_in"), sem("gate_up_in"), sem("bias_in"), sem("gla_gain_in"), sem("gain_in")
        xt_hi, xt_split = sem("xt_hi"), sem("xt_split")
        sel_ready = sem("sel_ready")
        small_done, glr_ready, ff_ready, cum_ready = sem("small_done"), sem("glr_ready"), sem("ff_ready"), sem("cum_ready")
        aux_done, proj_evac = sem("aux_done"), sem("proj_evac")
        la_ready, kdec_ready = sem("la_ready"), sem("kdec_ready")
        fox_logits, fox_max, fox_exp, fox_norm = sem("fox_logits"), sem("fox_max"), sem("fox_exp"), sem("fox_norm")
        fox_turned, fox_pT, fox_pv, fox_hi, fox_split = sem("fox_turned"), sem("fox_pT"), sem("fox_pv"), sem("fox_hi"), sem("fox_split")
        kv_done, state_done, o_read, o_evac = sem("kv_done"), sem("state_done"), sem("o_read"), sem("o_evac")
        rms_sqrt, silu_ready, o_gated = sem("rms_sqrt"), sem("silu_ready"), sem("o_gated")
        wout_done = sem("wout_done")
        oT_done, oT_hi, oT_split = sem("oT_done"), sem("oT_hi"), sem("oT_split")
        sig_ready, merged, m_hi_done, m_split = sem("sig_ready"), sem("merged"), sem("m_hi_done"), sem("m_split")
        x_in, ln_var, ln_sqrt, x1_ready, acc_ready = sem("x_in"), sem("ln_var"), sem("ln_sqrt"), sem("x1_ready"), sem("acc_ready")
        x1T_done, x1T_hi, x1T_split = sem("x1T_done"), sem("x1T_hi"), sem("x1T_split")
        q_evac, keys_in = sem("q_evac"), sem("keys_in")
        sc_done, sc_evac, sc_used = sem("sc_done"), sem("sc_evac"), sem("sc_used")
        best_ready, gate_exp, picks_ready, picks_turned, picks_evac = sem("best_ready"), sem("gate_exp"), sem("picks_ready"), sem("picks_turned"), sem("picks_evac")
        oh_made, oh_ready, gm_done, gm_evac = sem("oh_made"), sem("oh_ready"), sem("gm_done"), sem("gm_evac")
        gm_written = [sem("gm_written_a"), sem("gm_written_b")]
        act_written = [sem("act_written_a"), sem("act_written_b")]
        gates_in, act_in = sem("gates_in"), sem("act_in")
        gelu_done, wt_mul, wt_hi_done, wt_done = sem("gelu_done"), sem("wt_mul"), sem("wt_hi_done"), sem("wt_done")
        ffn_done, acc_done = sem("ffn_done"), sem("acc_done")
        ln2_in, ln2_var, ln2_sqrt, y_ready, y_out = sem("ln2_in"), sem("ln2_var"), sem("ln2_sqrt"), sem("y_ready"), sem("y_out")
        act_step, dve_step = sem("act_step"), sem("dve_step")

        n_proj = 9 * 4
        first_merge = n_proj
        first_wout = first_merge + 4 * KC
        first_query = first_wout + 8
        first_expert = first_query + HP
        gate_tiles = TOPK_TILES * TB
        bridge_tiles = gate_tiles + GATE_TILES * (NGB // 2)
        ahead_tiles = bridge_tiles + BRIDGE_TILES
        ahead_units = ahead_tiles // UNIT
        mixed_units = NUNIT - ahead_units
        first_gate = first_expert + gate_tiles
        first_bridge = first_expert + bridge_tiles
        first_mixed = first_expert + ahead_tiles
        first_tail = first_mixed + 2 * UNIT * mixed_units
        for n in (first_expert, first_gate, first_bridge, first_mixed, first_tail):
            assert n % RING == UNIT
        assert GATE_TILES == RING == BRIDGE_TILES and mixed_units % 2 == 0
        PT_UNITS = ["fq", "fk", "z", "fv", "gk", "sfx", "gq", "tot", "gv0", "gv1"]
        AUX = ["z", "sfx", "tot"]
        STREAMED = [name for name in PT_UNITS if name not in AUX] + ["gg0", "gg1"]

        def wait_product(eng, name, r):
            if name in AUX:
                eng.wait_ge(aux_done, 4 * AUX.index(name) + r + 1)
            else:
                by_column = name in ("fq", "fk", "gq")
                eng.wait_ge(quarter_used, 4 * STREAMED.index(name) + (r + 1 if by_column else 4))

        block = ctx.enter_context(nc.Block())

        @block.sync
        def _(sp):
            def load(n, src, width=QW):
                if n >= STAGE:
                    sp.wait_ge(split_done, n - STAGE + 1)
                sp.dma_start(stage[:, n % STAGE, 0:width], src).then_inc(landed[n % STAGE], 16)

            def load_x(j):
                sp.dma_start(xT_raw[:, 2 * j:2 * j + 2, :], xT[:, 2 * j:2 * j + 2, :]).then_inc(xt_in[j], 16)

            load_x(0)
            load_x(1)
            m = 0
            for n in range(first_expert):
                if n == 1:
                    load_x(2)
                    load_x(3)
                if first_merge <= n < first_wout and (n - first_merge) % 4 == 3:
                    load(n, fox_stream[(n - first_merge) // 4], 512)
                else:
                    load(n, mix_stream[m])
                    m += 1
            for k in range(gate_tiles):
                load(first_expert + k, expert_uT[k])

            def load_in_loop(n, k, src):
                sp.wait_ge(split_done, n - (STAGE - 1))
                sp.dma_start(stage[:, k % STAGE, :], src.rearrange("e p c -> p (e c)")).then_inc(landed[k % STAGE], 16)

            with sp.Fori(0, NGB // 2) as i:
                for k in range(GATE_TILES):
                    load_in_loop(i * RING + (first_gate + k), k,
                                 expert_uT[bass.ds(i * GATE_TILES + (gate_tiles + k), 1), :, :])
            for k in range(BRIDGE_TILES):
                load(first_bridge + k, expert_uT[bridge_tiles + k])
            with sp.Fori(0, mixed_units) as u:
                for k in range(UNIT):
                    load_in_loop(u * RING + (first_mixed + k), k, expert_uT[bass.ds(u * UNIT + (ahead_tiles + k), 1), :, :])
                for k in range(UNIT):
                    load_in_loop(u * RING + (first_mixed + UNIT + k), k, expert_v[bass.ds(u * UNIT + k, 1), :, :])
            with sp.Fori(0, (NUNIT - mixed_units) // 2) as i:
                for k in range(RING):
                    load_in_loop(i * RING + (first_tail + k), k, expert_v[bass.ds(i * RING + (UNIT * mixed_units + k), 1), :, :])
            for t in range(TB):
                sp.wait_ge(y_ready, t + 1)
                sp.dma_start(out[t * P:(t + 1) * P, :], acc[:, t, :]).then_inc(y_out, 16)
            sp.wait_ge(y_out, 16 * TB)

        @block.gpsimd
        def _(pool):
            steps = [0]

            def step(ins):
                steps[0] += 1
                ins.then_inc(pool_step, 1)
                pool.wait_ge(pool_step, steps[0])

            step(nc.gpsimd.memset(ident[:], 0.0))
            step(nc.gpsimd.memset(ident_b[:], 0.0))
            step(nc.gpsimd.memset(mask_b[:], 0.0))
            step(nc.gpsimd.memset(later[:], 1.0))
            step(nc.gpsimd.memset(head_sel_raw[:], 0.0))
            step(nc.gpsimd.memset(glrT[:], 1.0))
            step(nc.gpsimd.memset(chunk_ind, 0.0))
            step(nc.gpsimd.memset(eps_col, EPS))
            step(nc.gpsimd.affine_select(out=ident[:], in_=ident[:], compare_op=ALU.not_equal, fill=1.0, base=0,
                                         pattern=[[-1, P]], channel_multiplier=1))
            step(nc.gpsimd.affine_select(out=ident_b[:], in_=ident_b[:], compare_op=ALU.not_equal, fill=1.0, base=0,
                                         pattern=[[-1, P]], channel_multiplier=1))
            step(nc.gpsimd.affine_select(out=mask_b[:], in_=mask_b[:], compare_op=ALU.is_ge, fill=NEG, base=0,
                                         pattern=[[-1, P]], channel_multiplier=1))
            step(nc.gpsimd.affine_select(out=later[:], in_=later[:], compare_op=ALU.is_ge, fill=0.0, base=-1,
                                         pattern=[[-1, P]], channel_multiplier=1))
            step(nc.gpsimd.memset(later[CHUNK:P, 0:CHUNK], 0.0))
            step(nc.gpsimd.memset(chunk_ind[0:CHUNK, 0:1], 1.0))
            step(nc.gpsimd.memset(chunk_ind[CHUNK:P, 1:2], 1.0))
            step(nc.gpsimd.affine_select(out=head_sel_raw[:], in_=head_sel_raw[:], compare_op=ALU.not_equal, fill=-1.0, base=0,
                                         pattern=[[-1, FH], [0, P]], channel_multiplier=1))
            nc.gpsimd.iota(iota_n[:], pattern=[[1, NKEY]], base=0, channel_multiplier=0,
                           allow_small_or_imprecise_dtypes=True).then_inc(const_made, 1)

            def split_low(n, slot, width):
                pool.wait_ge(hi_done, n + 1)
                nc.gpsimd.tensor_tensor(w_lo[:, slot, 0:width], stage[:, slot % STAGE, 0:width],
                                        w_hi[:, slot, 0:width], ALU.subtract).then_inc(split_done, 1)

            for n in range(first_expert + UNIT):
                fox = first_merge <= n < first_wout and (n - first_merge) % 4 == 3
                split_low(n, n % RING, 512 if fox else QW)
            start = first_expert + UNIT
            total = first_expert + 2 * NKEY
            with pool.Fori(0, (total - start) // RING) as i:
                for k in range(RING):
                    split_low(i * RING + (start + k), k, QW)
            for n in range(start + (total - start) // RING * RING, total):
                split_low(n, n % RING, QW)

        @block.tensor
        def _(pe):
            mm, tr = nc.tensor.matmul, nc.tensor.transpose

            def mm3(dst, l_hi, l_lo, r_hi, r_lo, first, last):
                mm(dst, l_lo, r_hi, start=first, stop=False)
                mm(dst, l_hi, r_lo, start=False, stop=False)
                return mm(dst, l_hi, r_hi, start=False, stop=last)

            quarter = [0]

            def columns(dst, a_hi, a_lo, kc=KC):
                n = quarter[0]
                pe.wait_ge(split_done, n + 1)
                s = n % RING
                for k in range(kc):
                    c = slice(k * P, (k + 1) * P)
                    ins = mm3(dst, w_hi[:, s, c], w_lo[:, s, c], a_hi[:, k, :], a_lo[:, k, :], k == 0, k == kc - 1)
                quarter[0] += 1
                return ins.then_inc(quarter_used, 1)

            def rows(dsts, a_hi, a_lo):
                for q in range(4):
                    n = quarter[0]
                    pe.wait_ge(split_done, n + 1)
                    s = n % RING
                    for kk in range(2):
                        k = 2 * q + kk
                        c = slice(kk * 512, kk * 512 + 512)
                        for t in range(TB):
                            r = slice(t * P, (t + 1) * P)
                            ins = mm3(dsts[t][:], a_hi[:, k, r], a_lo[:, k, r], w_hi[:, s, c], w_lo[:, s, c],
                                      k == 0, k == KC - 1)
                    ins.then_inc(quarter_used, 1)
                    quarter[0] += 1
                return ins

            pe.wait_ge(small_in, 16)
            for k in range(KC):
                if k % 2 == 0:
                    pe.wait_ge(xt_in[k // 2], 16)
                ins = mm(bank[7][0:SMALL, :], small_sb[:, k, :], xT_raw[:, k, :], start=(k == 0), stop=(k == KC - 1))
            ins.then_inc(small_done, 1)

            for u, name in enumerate(PT_UNITS):
                b = bank[4 * (u % 2):4 * (u % 2) + 4]
                if u == 0:
                    pe.wait_ge(xt_split, KC)
                if u == 1:
                    pe.wait_ge(glr_ready, 1)
                    pe.wait_ge(ff_ready, 1)
                if u >= 2:
                    pe.wait_ge(proj_evac, 4 * (u - 1))
                if name in ("fq", "fk", "gq"):
                    for c in range(4):
                        columns(b[c][:], x_hi, x_lo)
                elif name == "z":
                    pe.wait_ge(gate_up_in, 32)
                    for t in range(TB):
                        mm(b[t][:], glrT[:, t * P:(t + 1) * P], gate_up_sb[:], start=True, stop=True).then_inc(aux_done, 1)
                elif name == "sfx":
                    pe.wait_ge(la_ready, TB)
                    pe.wait_ge(const_made, 1)
                    for t in range(TB):
                        mm(b[t][:], later[:], la[:, t, :], start=True, stop=True).then_inc(aux_done, 1)
                elif name == "tot":
                    for h in range(GH):
                        for t in range(TB):
                            ins = mm(b[h][:, 2 * t:2 * t + 2], la[:, t, h * GK:(h + 1) * GK], chunk_ind,
                                     start=True, stop=True)
                        ins.then_inc(aux_done, 1)
                else:
                    rows(b, x_hi, x_lo)

            NS = FH * TB
            pe.wait_ge(proj_evac, 4 * (len(PT_UNITS) - 1))
            pe.wait_ge(cum_ready, 1)
            pe.wait_ge(sel_ready, 1)

            def place(h):
                return 64 * (h % 2), h // 2

            for i in range(NS + 4):
                if i == 3:
                    pe.wait_ge(proj_evac, 4 * len(PT_UNITS))
                if i < NS:
                    h, qb = divmod(i, TB)
                    p0, c = place(h)
                    w = (qb + 1) * P
                    if i >= 4:
                        pe.wait_ge(fox_exp, i - 3)
                    L = fox_bank[i % 4]
                    mm(L[:, 0:w], fqT[p0:p0 + 64, c, qb * P:w], fkT[p0:p0 + 64, c, 0:w], start=True, stop=False)
                    mm(L[:, qb * P:w], ident_b[:], mask_b[:], start=False, stop=False)
                    mm(L[:, 0:w], head_sel[:, h, :], cum_lo[:, 0:w], start=False, stop=False)
                    mm(L[:, 0:w], head_sel[:, h, :], cum_hi[:, 0:w], start=False, stop=True).then_inc(fox_logits, 1)
                if 3 <= i < NS + 3:
                    s = i - 3
                    h, qb = divmod(s, TB)
                    pe.wait_ge(fox_norm, s + 1)
                    if s >= 2:
                        pe.wait_ge(fox_pT, s - 1)
                    for kb in range(qb + 1):
                        ins = tr(bank[3 + s % 2][:, kb * P:(kb + 1) * P], probs[:, s % 4, kb * P:(kb + 1) * P], ident[:])
                    ins.then_inc(fox_turned, 1)
                if i >= 4:
                    s = i - 4
                    h, qb = divmod(s, TB)
                    p0, c = place(h)
                    pe.wait_ge(fox_pT, s + 1)
                    if h % 2 == 0 and qb == 0 and c >= 2:
                        pe.wait_ge(fox_split, c - 1)
                    for kb in range(qb + 1):
                        ins = mm(bank[5 + c % 2][p0:p0 + 64, qb * P:(qb + 1) * P], fv[:, kb, h * FD:(h + 1) * FD],
                                 pT[:, s % 2, kb * P:(kb + 1) * P], start=(kb == 0), stop=(kb == qb))
                    ins.then_inc(fox_pv, 1)

            pe.wait_ge(kdec_ready, TB)
            pe.wait_ge(fox_pT, NS)
            for c in range(NCH + 1):
                if c == 1:
                    pe.wait_ge(fox_split, 4)
                for h in range(GH):
                    if c < NCH:
                        t, p0 = c // 2, CHUNK * (c % 2)
                        if c >= 1:
                            pe.wait_ge(state_done, 4 * (c - 1) + h + 1)
                        mm(bank[h][:, 0:GV], kdec[p0:p0 + CHUNK, t, h * GK:(h + 1) * GK],
                           gv[p0:p0 + CHUNK, t, h * GV:(h + 1) * GV], start=True, stop=True).then_inc(kv_done, 1)
                    if c >= 1:
                        r = c - 1
                        t, p0 = r // 2, CHUNK * (r % 2)
                        if r % 2 == 0 and t >= 2 and h == 0:
                            pe.wait_ge(o_evac, t - 1)
                        pe.wait_ge(state_done, 4 * r + h + 1)
                        mm(bank[4 + 2 * (t % 2) + h // 2][p0:p0 + CHUNK, (h % 2) * GV:(h % 2 + 1) * GV],
                           gqT[:, h, r * CHUNK:(r + 1) * CHUNK], state[:, r % 2, h, :], start=True, stop=True).then_inc(o_read, 1)
            rows(bank[0:4], x_hi, x_lo)
            pe.wait_ge(o_evac, TB)
            rows(bank[4:8], x_hi, x_lo)
            for v in range(KC):
                if v % 4 == 0:
                    pe.wait_ge(o_gated, v + 4)
                for t in range(TB):
                    ins = tr(bank[v][:, t * P:(t + 1) * P], o[:, t, v * P:(v + 1) * P], ident[:])
                ins.then_inc(oT_done, 1)
            for d in range(KC):
                b = bank[4 * (d % 2):4 * (d % 2) + 4]
                if d == 0:
                    pe.wait_ge(oT_split, 4)
                if d >= 2:
                    pe.wait_ge(merged, d - 1)
                columns(b[0][:], x_hi, x_lo)
                columns(b[1][:], x_hi, x_lo)
                if d == 0:
                    pe.wait_ge(oT_split, KC)
                columns(b[2][:], o_hi, o_lo)
                columns(b[3][:], f_hi, f_lo, 4)
            def turn_x1(t):
                pe.wait_ge(x1_ready, t + 1)
                for half in range(2):
                    for j in range(4):
                        k = 4 * half + j
                        ins = tr(bank[2 * t + half][:, j * P:(j + 1) * P], x1[:, t, k * P:(k + 1) * P], ident[:])
                    ins.then_inc(x1T_done, 1)

            pe.wait_ge(merged, KC - 1)
            for t in range(TB):
                r = slice(t * P, (t + 1) * P)
                for half in range(2):
                    for k in range(KC):
                        n = first_wout + 4 * half + k // 2
                        if t == 0:
                            pe.wait_ge(split_done, n + 1)
                            pe.wait_ge(m_split, k + 1)
                        c = slice(k % 2 * 512, k % 2 * 512 + 512)
                        ins = mm3(bank[2 * t + half][:], m_hi[:, k, r], m_lo_parts[k // 4][:, k % 4, r],
                                  w_hi[:, n % RING, c], w_lo[:, n % RING, c], k == 0, k == KC - 1)
                        if t == TB - 1 and k % 2 == 1:
                            ins.then_inc(quarter_used, 1)
                        elif k == KC - 1:
                            ins.then_inc(wout_done, 1)
                if t >= 1:
                    turn_x1(t - 1)
            turn_x1(TB - 1)
            quarter[0] += 8
            pe.wait_ge(x1T_split, 2 * TB)
            for c in range(HP):
                if c >= 4:
                    pe.wait_ge(q_evac, c - 3)
                columns(bank[4 + c % 4][:], x_hi, x_lo)
            pe.wait_ge(q_evac, HP)
            pe.wait_ge(keys_in, 16)

            def score_tile(slot, b, split, free):
                pe.wait_ge(split_done, split)
                pe.wait_ge(gelu_done, free)
                for c in range(KC):
                    w = slice(c * P, (c + 1) * P)
                    ins = mm3(bank[b][:], w_hi[:, slot, w], w_lo[:, slot, w], x_hi[:, c, :], x_lo[:, c, :],
                              c == 0, c == KC - 1)
                ins.then_inc(quarter_used, 1)

            tile = [0]

            def score_tiles(count):
                for _ in range(count):
                    n = first_expert + tile[0]
                    score_tile(n % RING, tile[0] % 4, n + 1, tile[0] + 1)
                    tile[0] += 1

            def key_scores(t):
                if t >= 2:
                    pe.wait_ge(picks_evac, t - 1)
                for g in range(4):
                    if t >= 1:
                        pe.wait_ge(sc_evac, 4 * (t - 1) + g + 1)
                    for j in range(4):
                        hp = 4 * g + j
                        ins = mm(bank[4 + g][:, j * P:(j + 1) * P], qT[:, hp, t * P:(t + 1) * P], keys[:, hp, :],
                                 start=True, stop=True)
                    ins.then_inc(sc_done, 1)

            pe.sem_inc(gelu_done, 4)
            key_scores(0)
            for t in range(TB):
                score_tiles(TOPK_TILES // 2)
                if t + 1 < TB:
                    key_scores(t + 1)
                score_tiles(TOPK_TILES // 2)
                pe.wait_ge(picks_ready, t + 1)
                pe.wait_ge(sc_evac, 4 * min(t + 2, TB))
                for a in range(3):
                    ins = tr(bank[4][:, a * P:(a + 1) * P], ijg[:, a, :], ident[:])
                ins.then_inc(picks_turned, 1)

            pe.wait_ge(picks_evac, TB)
            pe.sem_inc(gm_done, 2)
            with pe.Fori(0, NGB // 2) as i:
                for k in range(GATE_TILES):
                    score_tile((UNIT + k) % RING, k % 4, i * RING + (first_gate + k + 1),
                               i * RING + (gate_tiles + k + 1))
                    for g in (2 * k, 2 * k + 1):
                        pe.wait_ge(oh_ready, i * 16 + (g + 1))
                        pe.wait_ge(gm_evac, i * 16 + (g + 1))
                        for j in range(4):
                            dst = bank[4 + g % 4][:, j * P:(j + 1) * P]
                            for part in (2, 1, 0):
                                ins = mm(dst, oh_j[:, g % 2, :, j], oh_gate[:, g % 2, part, :, j],
                                         start=(part == 2), stop=(part == 0))
                        ins.then_inc(gm_done, 1)

            def combine(u, n, slot, w):
                pe.wait_ge(wt_done, u * UNIT + UNIT)
                pe.wait_ge(split_done, n + UNIT)
                for m in range(8):
                    t, half = divmod(m, 2)
                    pe.wait_ge(acc_done, u * 8 + (m + 1))
                    for k in range(UNIT):
                        r, c = slice(t * P, (t + 1) * P), slice(half * 512, half * 512 + 512)
                        ins = mm3(bank[4 + m % 4][:], wt_hi[:, w, k, r], wt_lo[:, w, k, r],
                                  w_hi[:, slot + k, c], w_lo[:, slot + k, c], k == 0, k == UNIT - 1)
                    ins.then_inc(ffn_done, 1)

            for k in range(BRIDGE_TILES):
                score_tile((UNIT + k) % RING, k % 4, first_bridge + k + 1, bridge_tiles + k + 1)
            pe.wait_ge(gm_evac, NGB * 8 + 4)
            pe.sem_inc(ffn_done, 8)
            with pe.Fori(0, mixed_units // 2) as i:
                for j in range(2):
                    for k in range(UNIT):
                        score_tile(UNIT + k, k, i * (2 * RING) + (first_mixed + RING * j + k + 1),
                                   i * (2 * UNIT) + (ahead_tiles + UNIT * j + k + 1))
                    combine(i * 2 + j, i * (2 * RING) + (first_mixed + RING * j + UNIT), 0, j)
            with pe.Fori(0, (NUNIT - mixed_units) // 2) as i:
                for j in range(2):
                    combine(i * 2 + (mixed_units + j), i * RING + (first_tail + UNIT * j), UNIT * (1 - j), j)

        @block.scalar
        def _(sc):
            act_f = nc.scalar.activation
            steps = [0]

            def step(ins):
                steps[0] += 1
                ins.then_inc(act_step, 1)
                sc.wait_ge(act_step, steps[0])

            next_hi = [0]

            def round_quarter(n, slot, width, land, free):
                sc.wait_ge(landed[slot % STAGE], land)
                if free is not None:
                    sc.wait_ge(quarter_used, free)
                act_f(w_hi[:, slot, 0:width], stage[:, slot % STAGE, 0:width], ACT.Copy).then_inc(hi_done, 1)

            def ahead(n):
                for m in range(next_hi[0], n + 1):
                    fox = first_merge <= m < first_wout and (m - first_merge) % 4 == 3
                    round_quarter(m, m % RING, 512 if fox else QW, 16 * (m // STAGE + 1),
                                  m - RING + 1 if m >= RING else None)
                next_hi[0] = max(next_hi[0], n + 1)

            sc.dma_start(small_sb[:], small_w).then_inc(small_in, 16)
            sc.dma_start(gate_up_sb[0:GRANK, :], gate_up).then_inc(gate_up_in, 16)
            sc.dma_start(gate_up_sb[GRANK:GRANK + 1, :], gate_bias).then_inc(gate_up_in, 16)
            sc.dma_start(f_bias, fox_f_bias.rearrange("a h -> h a")).then_inc(bias_in, 16)
            for k in range(KC):
                if k % 2 == 0:
                    sc.wait_ge(xt_in[k // 2], 16)
                if k == 4:
                    ahead(0)
                act_f(x_hi[:, k, :], xT_raw[:, k, :], ACT.Copy).then_inc(xt_hi, 1)
            ahead(3)
            sc.wait_ge(const_made, 1)
            sc.wait_ge(small_done, 1)
            act_f(glrT[0:GRANK, :], bank[7][32:32 + GRANK, :], ACT.Copy).then_inc(glr_ready, 1)
            sc.wait_ge(bias_in, 16)
            step(act_f(logf[:], bank[7][0:FH, :], ACT.Identity, bias=f_bias))
            step(act_f(logf2[:], logf[:], ACT.Abs))
            step(act_f(logf2[:], logf2[:], ACT.Exp, scale=-1.0))
            act_f(logf2[:], logf2[:], ACT.Ln, bias=1.0).then_inc(ff_ready, 1)
            act_f(head_sel[:], head_sel_raw[:], ACT.Copy).then_inc(sel_ready, 1)

            for u, name in enumerate(PT_UNITS):
                for r in range(4):
                    b = bank[4 * (u % 2) + r]
                    seen = 4 * sum(x not in AUX for x in PT_UNITS[:u])
                    ahead(seen + 5 + (r if name in ("fq", "fk", "gq") else 0 if name in AUX else 3))
                    wait_product(sc, name, r)
                    if name == "fq":
                        if r == 0:
                            sc.wait_ge(xt_split, KC)
                        act_f(fqT[:, r, :], b[:], ACT.Copy, scale=FD ** -0.5).then_inc(proj_evac, 1)
                    elif name == "fk":
                        act_f(fkT[:, r, :], b[:], ACT.Copy).then_inc(proj_evac, 1)
                    elif name == "fv":
                        act_f(fv[:, r, :], b[:], ACT.Copy).then_inc(proj_evac, 1)
                    elif name == "gk":
                        act_f(kdec[:, r, :], b[:], ACT.Copy).then_inc(proj_evac, 1)
                    elif name == "gq":
                        act_f(gqT[:, r, :], b[:], ACT.Copy, scale=GK ** -0.5).then_inc(proj_evac, 1)
                    elif name in ("gv0", "gv1"):
                        if r == 0 and name == "gv0":
                            sc.wait_ge(xt_split, KC)
                        c = 512 * (name == "gv1")
                        act_f(gv[:, r, c:c + 512], b[:], ACT.Copy).then_inc(proj_evac, 1)
                    elif name == "z":
                        if r == 0:
                            sc.wait_ge(cum_ready, 1)
                        if r >= 2:
                            sc.wait_ge(la_ready, r - 1)
                        step(act_f(la[:, r, :], b[:], ACT.Copy))
                        step(act_f(tmp[:, r % 2, :], la[:, r, :], ACT.Abs))
                        step(act_f(tmp[:, r % 2, :], tmp[:, r % 2, :], ACT.Exp, scale=-1.0))
                        act_f(tmp[:, r % 2, :], tmp[:, r % 2, :], ACT.Ln, bias=1.0).then_inc(proj_evac, 1)
                    elif name == "sfx":
                        if r == 0:
                            sc.wait_ge(la_ready, TB)
                        if r >= 2:
                            sc.wait_ge(kdec_ready, r - 1)
                        act_f(tmp[:, r % 2, :], b[:], ACT.Exp, scale=1.0 / GATE_TEMP).then_inc(proj_evac, 1)
                    elif name == "tot":
                        act_f(etot[:, r, :], b[:, 0:NCH], ACT.Exp, scale=1.0 / GATE_TEMP).then_inc(proj_evac, 1)

            NS = FH * TB
            ahead(first_merge - 8 + 5)
            sc.wait_ge(kdec_ready, TB)
            for i in range(NS + 5):
                if i < NS:
                    w = (i % TB + 1) * P
                    sc.wait_ge(fox_max, i + 1)
                    if i >= 4:
                        sc.wait_ge(fox_turned, i - 3)
                    act_f(probs[:, i % 4, 0:w], fox_bank[i % 4][:, 0:w], ACT.Exp, bias=negmax[:, i:i + 1],
                          accum_out=psums[:, i:i + 1]).then_inc(fox_exp, 1)
                if 3 <= i < NS + 3:
                    s = i - 3
                    w = (s % TB + 1) * P
                    sc.wait_ge(fox_turned, s + 1)
                    if s >= 2:
                        sc.wait_ge(fox_pv, s - 1)
                    act_f(pT[:, s % 2, 0:w], bank[3 + s % 2][:, 0:w], ACT.Copy).then_inc(fox_pT, 1)
                if i >= 5 and (i - 5) % 8 == 7:
                    c = (i - 5) // 8
                    sc.wait_ge(fox_pv, i - 4)
                    act_f(f_hi[:, c, :], bank[5 + c % 2][:], ACT.Copy).then_inc(fox_hi, 1)

            sc.dma_start(gla_gain_sb[:], gla_gain.broadcast_to([P, D])).then_inc(gla_gain_in, 16)
            for t in range(TB):
                sc.wait_ge(o_read, 8 * (t + 1))
                if t >= 1:
                    sc.wait_ge(o_evac, t)
                for half in range(2):
                    b = bank[4 + 2 * (t % 2) + half]
                    act_f(o[:, t, half * 512:half * 512 + 512], b[:], ACT.Copy)
                    for j in range(2):
                        ins = act_f(tmp[:, half, j * GV:(j + 1) * GV], b[:, j * GV:(j + 1) * GV], ACT.Square,
                                    accum_out=ss[:, 4 * t + 2 * half + j:4 * t + 2 * half + j + 1])
                ins.then_inc(o_evac, 1)
            sc.wait_ge(o_evac, TB)
            act_f(rs, ss, ACT.Sqrt, bias=eps_col, scale=1.0 / GV).then_inc(rms_sqrt, 1)
            for r in range(8):
                ahead(first_merge - 8 + 8 + 4 * (r // 4))
                wait_product(sc, f"gg{r // 4}", r % 4)
                if r >= 2:
                    sc.wait_ge(o_gated, r - 1)
                act_f(tmp[:, r % 2, :], bank[r][:], ACT.Silu).then_inc(silu_ready, 1)
            for v in range(KC):
                sc.wait_ge(oT_done, v + 1)
                act_f(o_hi[:, v, :], bank[v][:], ACT.Copy).then_inc(oT_hi, 1)
            def round_merged(d):
                sc.wait_ge(merged, d + 1)
                act_f(m_hi[:, d, :], sig_b[:, d % 2, :], ACT.Copy).then_inc(m_hi_done, 1)

            for d in range(KC):
                b = bank[4 * (d % 2):4 * (d % 2) + 4]
                if d >= 2:
                    sc.wait_ge(merged, d - 1)
                ahead(first_merge + 4 * d + 5)
                sc.wait_ge(quarter_used, first_merge + 4 * d + 1)
                act_f(sig_a[:, d % 2, :], b[0][:], ACT.Sigmoid).then_inc(sig_ready, 1)
                if d >= 1:
                    round_merged(d - 1)
                ahead(first_merge + 4 * d + 7)
                if d >= 2:
                    sc.wait_ge(m_split, d - 1)
                sc.wait_ge(quarter_used, first_merge + 4 * d + 2)
                act_f(sig_b[:, d % 2, :], b[1][:], ACT.Sigmoid).then_inc(sig_ready, 1)
            sc.wait_ge(quarter_used, first_wout)
            sc.dma_start(x1[:], x.rearrange("(t p) d -> p t d", p=P)).then_inc(x_in, 16)
            ahead(first_wout + 7)
            round_merged(KC - 1)
            sc.dma_start(keys[:], keysT).then_inc(keys_in, 16)
            sc.wait_ge(m_split, KC)
            sc.dma_start(ln_g1[:], ln1_gain.broadcast_to([P, D])).then_inc(gain_in, 16)
            sc.dma_start(ln_b1[:], ln1_bias.broadcast_to([P, D])).then_inc(gain_in, 16)

            def round_x1(t):
                for half in range(2):
                    sc.wait_ge(x1T_done, 2 * t + half + 1)
                    act_f(x_hi[:, 4 * half:4 * half + 4, t * P:(t + 1) * P],
                          bank[2 * t + half][:].rearrange("p (k t) -> p k t", k=4), ACT.Copy).then_inc(x1T_hi, 1)

            for t in range(TB):
                sc.wait_ge(ln_var, t + 1)
                act_f(sd[:, t:t + 1], mv[:, t, 1:2], ACT.Sqrt, bias=eps_col).then_inc(ln_sqrt, 1)
                if t >= 1:
                    round_x1(t - 1)
            ahead(first_query + 1)
            round_x1(TB - 1)
            for c in range(HP):
                ahead(first_query + c + 5)
                sc.wait_ge(quarter_used, first_query + c + 1)
                act_f(qT[:, c, :], bank[4 + c % 4][:], ACT.Copy).then_inc(q_evac, 1)
                if c < TB:
                    act_f(acc[:, c, :], x1[:, c, :], ACT.Copy, scale=ALPHA).then_inc(acc_ready, 1)

            def gelu_out(parity, b, n_used, turn):
                sc.wait_ge(quarter_used, n_used)
                if turn is not None:
                    sc.wait_ge(act_written[parity], turn)
                act_f(act_out[parity][:], bank[b][:], ACT.Gelu).then_inc(gelu_done, 1)

            def store_tile(tile, parity, dst):
                sc.wait_ge(gelu_done, tile + 5)
                sc.dma_start(dst, act_out[parity][:]).then_inc(act_written[parity], 16)

            tile = [0]

            def gelus(count):
                for _ in range(count):
                    t = tile[0]
                    gelu_out(t % 2, t % 4, first_expert + t + 1, 16 * (t // 2) if t >= 2 else None)
                    ahead(first_expert + t + 4)
                    store_tile(t, t % 2, act_dram[t // UNIT, :, t % UNIT, :])
                    tile[0] += 1

            def evac_scores(t):
                if t >= 1:
                    sc.wait_ge(sc_used, t)
                for g in range(4):
                    sc.wait_ge(sc_done, 4 * t + g + 1)
                    act_f(score[:, 4 * g:4 * g + 4, :],
                          bank[4 + g][:].rearrange("p (a n) -> p a n", a=4), ACT.Copy).then_inc(sc_evac, 1)

            sc.wait_ge(acc_ready, TB)
            evac_scores(0)
            for t in range(TB):
                gelus(TOPK_TILES // 2)
                if t + 1 < TB:
                    evac_scores(t + 1)
                gelus(TOPK_TILES // 2 - 1)
                sc.wait_ge(best_ready, t + 1)
                act_f(ijg[:, 2, :], ijg[:, 2, :], ACT.Exp).then_inc(gate_exp, 1)
                gelus(1)
                sc.wait_ge(picks_turned, t + 1)
                act_f(picks[:, :, t * P:(t + 1) * P],
                      bank[4][:, 0:3 * P].rearrange("p (a t) -> p a t", a=3), ACT.Copy).then_inc(picks_evac, 1)

            sc.sem_inc(gm_evac, 4)

            def gate_batches(i, first):
                for k in range(GATE_TILES):
                    half = k // 4
                    if not first and k % 4 == 0:
                        sc.wait_ge(gm_written[half], i * 16)
                    for g in (2 * k, 2 * k + 1):
                        sc.wait_ge(gm_done, i * 16 + (g + 3))
                        t0 = 4 * (g % 8)
                        act_f(gstage[half][:, :, t0:t0 + 4],
                              bank[4 + g % 4][:].rearrange("p (t i) -> p i t", t=4), ACT.Copy).then_inc(gm_evac, 1)
                    t = i * GATE_TILES + (gate_tiles + k)
                    n = i * RING + (first_gate + k)
                    gelu_out(k % 2, k % 4, n + 1, i * 64 + 16 * ((gate_tiles + k) // 2))
                    round_quarter(n + 4, k, QW, i * 32 + 16 * ((first_gate + k + 4) // STAGE + 1), n - 3)
                    u = i * 2 + (gate_tiles // UNIT + k // UNIT)
                    store_tile(t, k % 2, act_dram[bass.ds(u, 1), :, k % UNIT, :].rearrange("u p c -> p (u c)"))
                    if k % 4 == 3:
                        sc.wait_ge(gm_evac, i * 16 + (4 + 8 * (half + 1)))
                        sc.dma_start(gate_dram[:, :, bass.ds(i * 2 + half, 1), :].rearrange("u p b c -> p u (b c)"),
                                     gstage[half][:, :, :].rearrange("p (u c) t -> p u (c t)", c=UNIT))\
                            .then_inc(gm_written[half], 16)

            gate_batches(0, True)
            with sc.Fori(1, NGB // 2) as i:
                gate_batches(i, False)

            def load_unit(u):
                for parity in range(2):
                    sc.wait_ge(act_written[parity], u * 32 + 32)
                sc.dma_start(gates[:].rearrange("p b c t -> p (b c t)"),
                             gate_dram[bass.ds(u, 1), :, :, :].rearrange("u p b c -> p (u b c)")).then_inc(gates_in, 16)
                sc.dma_start(act[:].rearrange("p c t -> p (c t)"),
                             act_dram[bass.ds(u, 1), :, :, :].rearrange("u p c t -> p (u c t)")).then_inc(act_in, 16)

            for k in range(BRIDGE_TILES):
                t, n = bridge_tiles + k, first_bridge + k
                gelu_out(k % 2, k % 4, n + 1, 16 * (t // 2))
                round_quarter(None, k, QW, 16 * ((n + 4) // STAGE + 1), n - 3)
                store_tile(t, k % 2, act_dram[t // UNIT, :, t % UNIT, :])
                if k == 2:
                    for half in range(2):
                        sc.wait_ge(gm_written[half], 16 * NGB // 2)
                    load_unit(0)
            sc.dma_start(ln_g2[:], ln2_gain.broadcast_to([P, D])).then_inc(ln2_in, 16)
            sc.dma_start(ln_b2[:], ln2_bias.broadcast_to([P, D])).then_inc(ln2_in, 16)

            def round_values(n_land, slot, used):
                sc.wait_ge(ffn_done, used)
                for k in range(UNIT):
                    round_quarter(None, slot + k, QW, n_land, None)

            with sc.Fori(0, mixed_units) as u:
                sc.wait_ge(wt_done, u * UNIT + UNIT)
                load_unit(u + 1)
                sc.wait_ge(quarter_used, u * UNIT + (first_mixed))
                round_values(u * 32 + 16 * ((first_mixed + UNIT) // STAGE + 1), 0, u * 8 + 8)
                for k in range(UNIT):
                    t = u * UNIT + (ahead_tiles + k)
                    gelu_out(k % 2, k, t + (first_expert + 1), u * 32 + 16 * ((ahead_tiles + k) // 2))
                    round_quarter(None, UNIT + k, QW, u * 32 + 16 * ((first_mixed + RING + k) // STAGE + 1),
                                  t + (first_expert + 1))
                    store_tile(t, k % 2, act_dram[bass.ds(u + ahead_units, 1), :, k, :].rearrange("u p c -> p (u c)"))

            def tail_unit(u, j, land):
                sc.wait_ge(wt_done, u * UNIT + UNIT)
                load_unit(u + 1)
                round_values(land, UNIT * j, u * 8 + 8)

            with sc.Fori(0, (NUNIT - mixed_units) // 2 - 1) as i:
                for j in range(2):
                    tail_unit(i * 2 + (mixed_units + j), j, i * 32 + 16 * ((first_tail + UNIT * (j + 1)) // STAGE + 1))
            tail_unit(NUNIT - 2, 0, 16 * ((first_tail + UNIT * (NUNIT - mixed_units - 1)) // STAGE + 1))
            for t in range(TB):
                sc.wait_ge(ln2_var, t + 1)
                act_f(sd[:, t:t + 1], mv[:, t, 1:2], ACT.Sqrt, bias=eps_col).then_inc(ln2_sqrt, 1)

        @block.vector
        def _(dve):
            v = nc.vector
            steps = [0]

            def step(ins):
                steps[0] += 1
                ins.then_inc(dve_step, 1)
                dve.wait_ge(dve_step, steps[0])

            for k in range(KC):
                dve.wait_ge(xt_hi, k + 1)
                v.tensor_tensor(x_lo[:, k, :], xT_raw[:, k, :], x_hi[:, k, :], ALU.subtract).then_inc(xt_split, 1)
            step(v.memset(zero_row[:], 0.0))
            dve.wait_ge(ff_ready, 1)
            step(v.scalar_tensor_tensor(out=logf[:], in0=logf[:], scalar=0.0, in1=logf2[:], op0=ALU.min, op1=ALU.subtract))
            step(v.tensor_tensor_scan(cum[:], logf[:], zero_row[:], 0.0, ALU.add, ALU.add))
            step(v.tensor_copy(cum_hi[:], cum[:]))
            v.tensor_tensor(cum_lo[:], cum[:], cum_hi[:], ALU.subtract).then_inc(cum_ready, 1)
            for r in range(TB):
                dve.wait_ge(proj_evac, 8 + r + 1)
                v.scalar_tensor_tensor(out=la[:, r, :], in0=la[:, r, :], scalar=0.0, in1=tmp[:, r % 2, :],
                                       op0=ALU.min, op1=ALU.subtract).then_inc(la_ready, 1)
            for r in range(TB):
                dve.wait_ge(proj_evac, 20 + r + 1)
                v.tensor_tensor(kdec[:, r, :], kdec[:, r, :], tmp[:, r % 2, :], ALU.mult).then_inc(kdec_ready, 1)
            NS = FH * TB
            for i in range(NS + 5):
                if i < NS:
                    w = (i % TB + 1) * P
                    dve.wait_ge(fox_logits, i + 1)
                    v.tensor_reduce(negmax[:, i:i + 1], fox_bank[i % 4][:, 0:w], AX.X, ALU.max, negate=True).then_inc(fox_max, 1)
                if 1 <= i < NS + 1:
                    s = i - 1
                    w = (s % TB + 1) * P
                    dve.wait_ge(fox_exp, s + 1)
                    step(v.reciprocal(recips[:, s:s + 1], psums[:, s:s + 1]))
                    v.tensor_scalar(probs[:, s % 4, 0:w], probs[:, s % 4, 0:w], recips[:, s:s + 1], None,
                                    ALU.mult).then_inc(fox_norm, 1)
                if i >= 5 and (i - 5) % 8 == 7:
                    c = (i - 5) // 8
                    dve.wait_ge(fox_hi, c + 1)
                    v.tensor_tensor(f_lo[:, c, :], bank[5 + c % 2][:], f_hi[:, c, :], ALU.subtract).then_inc(fox_split, 1)
            for c in range(NCH):
                for h in range(GH):
                    dve.wait_ge(kv_done, 4 * c + h + 1)
                    if c >= 2:
                        dve.wait_ge(o_read, 4 * (c - 2) + h + 1)
                    if c == 0:
                        v.tensor_copy(state[:, 0, h, :], bank[h][:, 0:GV]).then_inc(state_done, 1)
                    else:
                        dve.wait_ge(state_done, 4 * (c - 1) + h + 1)
                        v.scalar_tensor_tensor(out=state[:, c % 2, h, :], in0=state[:, 1 - c % 2, h, :],
                                               scalar=etot[:, h, c:c + 1], in1=bank[h][:, 0:GV],
                                               op0=ALU.mult, op1=ALU.add).then_inc(state_done, 1)
            dve.wait_ge(rms_sqrt, 1)
            step(v.reciprocal(rs, rs))
            dve.wait_ge(gla_gain_in, 16)
            for t in range(TB):
                for h in range(GH):
                    c = slice(h * GV, (h + 1) * GV)
                    ins = v.scalar_tensor_tensor(out=o[:, t, c], in0=o[:, t, c], scalar=rs[:, 4 * t + h:4 * t + h + 1],
                                                 in1=gla_gain_sb[:, c], op0=ALU.mult, op1=ALU.mult)
            step(ins)
            for r in range(8):
                dve.wait_ge(silu_ready, r + 1)
                half, t = divmod(r, TB)
                c = slice(half * 512, half * 512 + 512)
                v.tensor_tensor(o[:, t, c], o[:, t, c], tmp[:, r % 2, :], ALU.mult).then_inc(o_gated, 1)
            for k in range(KC):
                dve.wait_ge(oT_hi, k + 1)
                v.tensor_tensor(o_lo[:, k, :], bank[k][:], o_hi[:, k, :], ALU.subtract).then_inc(oT_split, 1)
            def split_merged(d):
                dve.wait_ge(m_hi_done, d + 1)
                v.tensor_tensor(m_lo_parts[d // 4][:, d % 4, :], sig_b[:, d % 2, :], m_hi[:, d, :],
                                ALU.subtract).then_inc(m_split, 1)

            for d in range(KC):
                b = bank[4 * (d % 2):4 * (d % 2) + 4]
                dve.wait_ge(sig_ready, 2 * d + 2)
                dve.wait_ge(quarter_used, first_merge + 4 * d + 4)
                v.tensor_tensor(sig_a[:, d % 2, :], sig_a[:, d % 2, :], b[3][:], ALU.mult)
                step(v.tensor_tensor(sig_b[:, d % 2, :], sig_b[:, d % 2, :], b[2][:], ALU.mult))
                v.tensor_tensor(sig_b[:, d % 2, :], sig_a[:, d % 2, :], sig_b[:, d % 2, :], ALU.add).then_inc(merged, 1)
                if d >= 1:
                    split_merged(d - 1)
            split_merged(KC - 1)

            def norm_stats(src, t):
                for half in range(2):
                    ins = v.bn_stats(stats[:, 12 * t + 6 * half:12 * t + 6 * half + 6], src[:, t, half * 512:half * 512 + 512])
                step(ins)
                return v.bn_aggr(mv[:, t, :], stats[:, 12 * t:12 * t + 12])

            def norm_apply(src, t, gain, bias, var, sqrt, done):
                dve.wait_ge(var, t + 1)
                v.scalar_tensor_tensor(out=src[:, t, :], in0=src[:, t, :], scalar=mv[:, t, 0:1], in1=gain[:],
                                       op0=ALU.subtract, op1=ALU.mult)
                dve.wait_ge(sqrt, t + 1)
                step(v.reciprocal(sd[:, t:t + 1], sd[:, t:t + 1]))
                v.scalar_tensor_tensor(out=src[:, t, :], in0=src[:, t, :], scalar=sd[:, t:t + 1], in1=bias[:],
                                       op0=ALU.mult, op1=ALU.add).then_inc(done, 1)

            def split_x1(t):
                for half in range(2):
                    dve.wait_ge(x1T_hi, 2 * t + half + 1)
                    k = slice(4 * half, 4 * half + 4)
                    v.tensor_tensor(x_lo[:, k, t * P:(t + 1) * P], bank[2 * t + half][:].rearrange("p (k t) -> p k t", k=4),
                                    x_hi[:, k, t * P:(t + 1) * P], ALU.subtract).then_inc(x1T_split, 1)

            dve.wait_ge(x_in, 16)
            dve.wait_ge(gain_in, 32)
            for t in range(TB):
                for half in range(2):
                    if t < TB - 1:
                        dve.wait_ge(wout_done, 2 * t + half + 1)
                    else:
                        dve.wait_ge(quarter_used, first_wout + 4 * half + 4)
                    c = slice(half * 512, half * 512 + 512)
                    ins = v.scalar_tensor_tensor(out=x1[:, t, c], in0=x1[:, t, c], scalar=ALPHA, in1=bank[2 * t + half][:],
                                                 op0=ALU.mult, op1=ALU.add)
                step(ins)
                norm_stats(x1, t).then_inc(ln_var, 1)
                norm_apply(x1, t, ln_g1, ln_b1, ln_var, ln_sqrt, x1_ready)
                if t >= 1:
                    split_x1(t - 1)
            split_x1(TB - 1)

            square = [P, PH, TOPK, TOPK]
            dve.wait_ge(acc_ready, TB)
            v.tensor_copy(iota_o[:], iota_n[:, 0:TOPK])
            for t in range(TB):
                dve.wait_ge(sc_evac, 4 * t + 4)

                def top16(vals, idx, src, rows_n):
                    for a in range(rows_n):
                        ins = v.max(vals[:, a, 0:8], src[:, a, :])
                    step(ins)
                    for a in range(rows_n):
                        ins = v.max_index(idx[:, a, 0:8], vals[:, a, 0:8], src[:, a, :])
                    step(ins)
                    for a in range(rows_n):
                        ins = v.match_replace(src[:, a, :], vals[:, a, 0:8], src[:, a, :], NEG_REPLACE)
                    step(ins)
                    for a in range(rows_n):
                        ins = v.max(vals[:, a, 8:16], src[:, a, :])
                    step(ins)
                    for a in range(rows_n):
                        ins = v.max_index(idx[:, a, 8:16], vals[:, a, 8:16], src[:, a, :])
                    return ins

                top16(top_v, top_i, score, HP).then_inc(sc_used, 1)
                dve.wait_ge(sc_used, t + 1)
                v.tensor_copy(top_if[:], top_i[:])
                tv = top_v[:].rearrange("p (h s) k -> p h s k", s=2)
                step(v.tensor_tensor(
                    cand[:].rearrange("p h (a b) -> p h a b", a=TOPK),
                    tv[:, :, 0, :].unsqueeze(3).broadcast_to(square), tv[:, :, 1, :].unsqueeze(2).broadcast_to(square), ALU.add))
                step(top16(best, pos, cand, PH))
                if t >= 1:
                    dve.wait_ge(picks_turned, t)
                v.tensor_tensor(ijg[:, 2, :].rearrange("p (h k) -> p h k", h=PH), best[:],
                                best[:, :, 0:1].broadcast_to([P, PH, TOPK]), ALU.subtract).then_inc(best_ready, 1)
                v.tensor_scalar(pos_i[:, 0, :, :], pos[:], 4, None, ALU.logical_shift_right)
                step(v.tensor_scalar(pos_i[:, 1, :, :], pos[:], TOPK - 1, None, ALU.bitwise_and))
                step(v.tensor_copy(pos_f[:], pos_i[:]))
                ti = top_if[:].rearrange("p (h s) k -> p h s k", s=2)
                eq = cand[:].rearrange("p h (k o) -> p h k o", o=TOPK)
                for a in range(2):
                    step(v.tensor_tensor(eq, pos_f[:, a, :, :].unsqueeze(3).broadcast_to(square),
                                         iota_o[:].unsqueeze(1).unsqueeze(1).broadcast_to(square), ALU.is_equal))
                    step(v.tensor_tensor(eq, eq, ti[:, :, a, :].unsqueeze(2).broadcast_to(square), ALU.mult))
                    step(v.tensor_reduce(ijg[:, a, :].rearrange("p (h k) -> p h k", h=PH), eq, AX.X, ALU.add))
                dve.wait_ge(gate_exp, t + 1)
                gx = ijg[:, 2, :].rearrange("p (h k) -> p h k", h=PH)
                step(v.tensor_reduce(gsum, gx, AX.X, ALU.add))
                step(v.reciprocal(grec, gsum))
                v.tensor_tensor(gx, gx, grec.unsqueeze(2).broadcast_to([P, PH, TOPK]), ALU.mult).then_inc(picks_ready, 1)

            dve.wait_ge(picks_evac, TB)
            v.tensor_copy(iota_g[:], iota_n[:].unsqueeze(2).broadcast_to([P, NKEY, GT]))
            v.tensor_copy(pick_keys[:], picks[:, 0:2, :])
            step(v.tensor_copy(gate_parts[:, 0, :], picks[:, 2, :]))
            step(v.tensor_tensor(picks[:, 2, :], picks[:, 2, :], gate_parts[:, 0, :], ALU.subtract))
            step(v.tensor_copy(gate_parts[:, 1, :], picks[:, 2, :]))
            step(v.tensor_tensor(gate_parts[:, 2, :], picks[:, 2, :], gate_parts[:, 1, :], ALU.subtract))
            group = [P, NKEY, GT]
            with dve.Fori(0, NGB // 2) as i:
                for g in range(16):
                    dve.wait_ge(gm_done, i * 16 + (g + 1))
                    tok = bass.ds(i * 64 + GT * g, GT)
                    v.tensor_tensor(oh_i[:, g % 2], iota_g[:], pick_keys[:, 0, tok].unsqueeze(1).broadcast_to(group),
                                    ALU.is_equal).then_inc(oh_made, 1)
                    v.tensor_tensor(oh_j[:, g % 2], iota_g[:], pick_keys[:, 1, tok].unsqueeze(1).broadcast_to(group),
                                    ALU.is_equal)
                    dve.wait_ge(oh_made, i * 16 + (g + 1))
                    for part in range(3):
                        ins = v.tensor_tensor(oh_gate[:, g % 2, part], oh_i[:, g % 2],
                                              gate_parts[:, part, tok].unsqueeze(1).broadcast_to(group), ALU.mult)
                    ins.then_inc(oh_ready, 1)

            def weigh(u, k, w):
                n = u * UNIT + (k + 1)
                if k == 0:
                    dve.wait_ge(gates_in, u * 16 + 16)
                    dve.wait_ge(act_in, u * 16 + 16)
                a = act[:, k, :]
                v.tensor_tensor(a.rearrange("p (b t) -> p b t", b=NGB), a.rearrange("p (b t) -> p b t", b=NGB),
                                gates[:, :, k, :], ALU.mult).then_inc(wt_mul, 1)
                dve.wait_ge(wt_mul, n)
                v.tensor_copy(wt_hi[:, w, k, :], a).then_inc(wt_hi_done, 1)
                dve.wait_ge(wt_hi_done, n)
                v.tensor_tensor(wt_lo[:, w, k, :], a, wt_hi[:, w, k, :], ALU.subtract).then_inc(wt_done, 1)

            def add_out(u, m):
                t, half = divmod(m, 2)
                c = slice(half * 512, half * 512 + 512)
                dve.wait_ge(acc_done, u * 8 + (m + 1))
                dve.wait_ge(ffn_done, u * 8 + (m + 9))
                v.tensor_tensor(acc[:, t, c], acc[:, t, c], bank[4 + m % 4][:], ALU.add).then_inc(acc_done, 1)

            def unit_out(u, w):
                for m in range(8):
                    add_out(u, m)
                    if w is not None and 2 <= m < 2 + UNIT:
                        if m == 2:
                            dve.wait_ge(ffn_done, u * 8 + 8)
                        weigh(u + 1, m - 2, w)

            for k in range(UNIT):
                weigh(0, k, 0)
            dve.sem_inc(acc_done, 4)
            with dve.Fori(0, NUNIT // 2 - 1) as i:
                unit_out(i * 2, 1)
                unit_out(i * 2 + 1, 0)
            unit_out(NUNIT - 2, 1)
            dve.wait_ge(ln2_in, 32)
            for t in range(TB):
                add_out(NUNIT - 1, 2 * t)
                add_out(NUNIT - 1, 2 * t + 1)
                dve.wait_ge(acc_done, 8 * (NUNIT - 1) + 4 + 2 * t + 2)
                norm_stats(acc, t).then_inc(ln2_var, 1)
                norm_apply(acc, t, ln_g2, ln_b2, ln2_var, ln2_sqrt, y_ready)


def kernel(**inputs):
    import numpy as np
    import concourse.bacc as bacc
    from concourse.bass_utils import run_bass_kernel_spmd

    def of(name):
        return np.ascontiguousarray(inputs[name])[0]

    x = of("x")
    w_in = of("w_in")
    widths = [512, 512, 512, FH, GH * GK, GH * GK, D, D, GRANK, D, D]
    at = [sum(widths[:i]) for i in range(len(widths))]
    fq, fk, fv, ff, gq, gk, gv, gg, glr, mga, mgb = [w_in[:, a:a + n] for a, n in zip(at, widths)]

    def columns(w, c):
        k = w.shape[0] // P
        return w[:, c * P:(c + 1) * P].reshape(k, P, P).transpose(1, 0, 2).reshape(P, k * P)

    def rows(w, half, q):
        return w[2 * P * q:2 * P * (q + 1), 512 * half:512 * half + 512].reshape(2, P, 512).transpose(1, 0, 2).reshape(P, 1024)

    quarters = [columns(fq, c) for c in range(4)] + [columns(fk, c) for c in range(4)]
    quarters += [rows(fv, 0, q) for q in range(4)] + [rows(gk, 0, q) for q in range(4)]
    quarters += [columns(gq, c) for c in range(4)]
    quarters += [rows(w, half, q) for w in (gv, gg) for half in range(2) for q in range(4)]
    w_gla, w_fox, w_out = of("w_out_gla"), of("w_out_fox"), of("w_out")
    for d in range(D // P):
        quarters += [columns(mga, d), columns(mgb, d), columns(w_gla, d)]
    quarters += [rows(w_out, half, q) for half in range(2) for q in range(4)]
    w_query = of("peer_w_query").reshape(D, HP * P)
    quarters += [columns(w_query, c) for c in range(HP)]

    arrays = {
        "xT": x.reshape(S, KC, P).transpose(2, 1, 0),
        "x": x.reshape(S, D),
        "mix_stream": np.stack(quarters),
        "fox_stream": np.stack([columns(w_fox, d) for d in range(D // P)]),
        "small_w": np.concatenate([ff, ff, ff, ff, glr], axis=1).reshape(KC, P, SMALL).transpose(1, 0, 2),
        "fox_f_bias": of("fox_f_bias")[None],
        "gate_up": of("gla_gate_up"),
        "gate_bias": of("gla_gate_bias")[None],
        "gla_gain": of("gla_norm_gain").reshape(1, D),
        "ln1_gain": of("ln1_gain")[None], "ln1_bias": of("ln1_bias")[None],
        "ln2_gain": of("ln2_gain")[None], "ln2_bias": of("ln2_bias")[None],
        "keysT": of("peer_sub_keys").reshape(HP, NKEY, P).transpose(2, 0, 1),
        "expert_uT": of("peer_expert_u").reshape(NKEY, NKEY, KC, P).transpose(0, 3, 2, 1).reshape(NKEY, P, D),
        "expert_v": of("peer_expert_v").reshape(NKEY, NKEY, D),
    }
    arrays = {k: np.ascontiguousarray(a) for k, a in arrays.items()}
    nc = bacc.Bacc("TRN2", target_bir_lowering=False, num_devices=1)
    args = {k: nc.dram_tensor(f"in_{k}", a.shape, mybir.dt.from_np(a.dtype), kind="ExternalInput").ap()
            for k, a in arrays.items()}
    out = nc.dram_tensor("out_0", (S, D), F32, kind="ExternalOutput").ap()
    build(nc, out=out, **args)
    r = run_bass_kernel_spmd(nc, [{f"in_{k}": a for k, a in arrays.items()}], core_ids=[0])
    return r.results[0]["out_0"].reshape(1, S, D)
```
